# Optimizing a Trainium2 kernel written in Bass

```python
import math
import jax, jax.numpy as jnp
from jax import lax
import numpy as np

D_MODEL = 2048
BATCH = 1
SEQ = 256
DEPTH = 2

GRID_W = 64
CTX_LEN = 256
HEAD_DIM = 128
N_GROUPS = 4
GROUP_HEADS = D_MODEL // (N_GROUPS * HEAD_DIM)
GROUP_WIDTH = GROUP_HEADS * HEAD_DIM
MIX_WIDTH = N_GROUPS * GROUP_WIDTH
KV_HEADS = 2
KV_WIDTH = KV_HEADS * HEAD_DIM
DIFF_DIM = HEAD_DIM // 2
WINDOW = 128
Q_BLOCK = 128
NA_WIN_H = 8
NA_WIN_W = 16
NA_COL_BLOCK = 16
NA_KEY_COLS = NA_COL_BLOCK + NA_WIN_W
ROPE_THETA = 10000.0
EPS = 1e-6
NEG_INF = -1e30

IN_SIZES = (GROUP_WIDTH, GROUP_WIDTH, GROUP_WIDTH,
            GROUP_WIDTH, KV_WIDTH, KV_WIDTH,
            GROUP_WIDTH, GROUP_WIDTH, GROUP_WIDTH,
            GROUP_WIDTH, KV_WIDTH, KV_WIDTH,
            MIX_WIDTH)
IN_WIDTH = sum(IN_SIZES)


def rms_norm(x, g):
    xf = x.astype(jnp.float32)
    y = xf * lax.rsqrt(jnp.mean(xf * xf, axis=-1, keepdims=True) + EPS)
    return (y * g.astype(jnp.float32)).astype(x.dtype)

def axial_rope_tables(n_tokens, dim, dtype):
    t = jnp.arange(n_tokens)
    row = (t // GRID_W).astype(jnp.float32)
    col = (t % GRID_W).astype(jnp.float32)
    n_freq = dim // 4
    inv = ROPE_THETA ** (-jnp.arange(n_freq, dtype=jnp.float32) / n_freq)
    ang = jnp.concatenate([row[:, None] * inv, col[:, None] * inv], axis=-1)
    return jnp.cos(ang).astype(dtype), jnp.sin(ang).astype(dtype)

def apply_rope(x, cos, sin):
    h = x.shape[-1] // 2
    x1, x2 = x[..., :h], x[..., h:]
    return jnp.concatenate([x1 * cos - x2 * sin, x2 * cos + x1 * sin], axis=-1)

def to_heads(t, n_heads, dim):
    b, s, _ = t.shape
    return t.reshape(b, s, n_heads, dim).transpose(0, 2, 1, 3)

def from_heads(t):
    b, h, s, d = t.shape
    return t.transpose(0, 2, 1, 3).reshape(b, s, h * d)

def diff_attention(q_lat, k_lat, v_lat, q_ctx, k_ctx, v_ctx, lam, subln_g, lambda_init, rope, with_ctx):
    cos, sin = rope
    b, s, _ = q_lat.shape
    H = GROUP_HEADS
    nblk = s // Q_BLOCK
    scale = DIFF_DIM ** -0.5

    def split2(t):
        n = t.shape[1]
        return t.reshape(b, n, H, 2, DIFF_DIM).transpose(0, 2, 3, 1, 4)

    ql = apply_rope(split2(q_lat), cos, sin)
    kl = apply_rope(split2(k_lat), cos, sin)
    kc = split2(k_ctx)
    vl, vc = to_heads(v_lat, H, HEAD_DIM), to_heads(v_ctx, H, HEAD_DIM)
    k_all = jnp.concatenate([kc, kl], axis=3)
    v_all = jnp.concatenate([vc, vl], axis=2)

    def attend(q, k, v):
        p = jax.nn.softmax(jnp.einsum('bhpqd,bhpkd->bhpqk', q, k).astype(jnp.float32) * scale, axis=-1)
        a = p[:, :, 0] - lam * p[:, :, 1]
        return jnp.einsum('bhqk,bhkd->bhqd', a.astype(v.dtype), v)

    qb = jnp.moveaxis(ql.reshape(b, H, 2, nblk, Q_BLOCK, DIFF_DIM), 3, 0)
    ob = lax.map(lambda qq: attend(qq, k_all, v_all), qb)
    o_lat = jnp.moveaxis(ob, 0, 2).reshape(b, H, s, HEAD_DIM)

    def post(o):
        return from_heads(rms_norm(o, subln_g) * (1.0 - lambda_init))

    if not with_ctx:
        return post(o_lat), None
    return post(o_lat), post(attend(split2(q_ctx), kc, vc))

def _band(t, nblk, side):
    b, hk, s, d = t.shape
    tp = jnp.pad(t, ((0, 0), (0, 0), (side * Q_BLOCK, side * Q_BLOCK), (0, 0)))
    tp = tp.reshape(b, hk, nblk + 2 * side, Q_BLOCK, d)
    return jnp.concatenate([tp[:, :, j:j + nblk] for j in range(2 * side + 1)], axis=3)

def window_attention(q_lat, k_lat, v_lat, q_ctx, k_ctx, v_ctx, sink, rope, with_ctx):
    cos, sin = rope
    b, s, _ = q_lat.shape
    L = k_ctx.shape[1]
    g = GROUP_HEADS // KV_HEADS
    nblk = s // Q_BLOCK
    side = WINDOW // Q_BLOCK
    nk = (2 * side + 1) * Q_BLOCK
    scale = HEAD_DIM ** -0.5
    ql = apply_rope(to_heads(q_lat, GROUP_HEADS, HEAD_DIM), cos, sin).reshape(b, KV_HEADS, g, nblk, Q_BLOCK, HEAD_DIM)
    kl = apply_rope(to_heads(k_lat, KV_HEADS, HEAD_DIM), cos, sin)
    vl = to_heads(v_lat, KV_HEADS, HEAD_DIM)
    kc, vc = to_heads(k_ctx, KV_HEADS, HEAD_DIM), to_heads(v_ctx, KV_HEADS, HEAD_DIM)
    kb, vb = _band(kl, nblk, side), _band(vl, nblk, side)
    n = np.arange(nblk)[:, None, None]
    t = np.arange(Q_BLOCK)[None, :, None]
    j = np.arange(nk)[None, None, :]
    qpos = n * Q_BLOCK + t
    kpos = (n - side) * Q_BLOCK + j
    valid = (np.abs(kpos - qpos) <= WINDOW) & (kpos >= 0) & (kpos < s)
    sink_hg = sink.astype(jnp.float32).reshape(KV_HEADS, g)
    s_band = jnp.where(valid, jnp.einsum('bkgnqd,bknjd->bkgnqj', ql, kb).astype(jnp.float32) * scale, NEG_INF)
    s_ctx = jnp.einsum('bkgnqd,bkld->bkgnql', ql, kc).astype(jnp.float32) * scale
    s_sink = jnp.broadcast_to(sink_hg[None, :, :, None, None, None], s_ctx.shape[:-1] + (1,))
    p = jax.nn.softmax(jnp.concatenate([s_band, s_ctx, s_sink], axis=-1), axis=-1).astype(vl.dtype)
    o = (jnp.einsum('bkgnqj,bknjd->bkgnqd', p[..., :nk], vb)
         + jnp.einsum('bkgnql,bkld->bkgnqd', p[..., nk:nk + L], vc))
    o_lat = from_heads(o.reshape(b, GROUP_HEADS, s, HEAD_DIM))
    if not with_ctx:
        return o_lat, None
    qc = to_heads(q_ctx, GROUP_HEADS, HEAD_DIM).reshape(b, KV_HEADS, g, L, HEAD_DIM)
    sc = jnp.einsum('bkgqd,bkld->bkgql', qc, kc).astype(jnp.float32) * scale
    sink_c = jnp.broadcast_to(sink_hg[None, :, :, None, None], sc.shape[:-1] + (1,))
    pc = jax.nn.softmax(jnp.concatenate([sc, sink_c], axis=-1), axis=-1)[..., :L].astype(vc.dtype)
    oc = jnp.einsum('bkgql,bkld->bkgqd', pc, vc).reshape(b, GROUP_HEADS, L, HEAD_DIM)
    return o_lat, from_heads(oc)

def neighborhood_attention(q_lat, k_lat, v_lat, q_ctx, k_ctx, v_ctx, rpb, with_ctx):
    b, s, _ = q_lat.shape
    rows = s // GRID_W
    H = GROUP_HEADS
    scale = HEAD_DIM ** -0.5
    wr = min(NA_WIN_H, rows)
    n_cb = GRID_W // NA_COL_BLOCK
    K = wr * NA_KEY_COLS
    r = np.arange(rows)
    key_rows = np.clip(r - wr // 2, 0, rows - wr)[:, None] + np.arange(wr)
    cb = np.arange(n_cb)
    key_cols = (np.clip(cb * NA_COL_BLOCK - NA_WIN_W // 2, 0, GRID_W - NA_KEY_COLS)[:, None]
                + np.arange(NA_KEY_COLS))
    qcol = cb[:, None] * NA_COL_BLOCK + np.arange(NA_COL_BLOCK)
    cstart = np.clip(qcol - NA_WIN_W // 2, 0, GRID_W - NA_WIN_W)
    key_idx = (key_rows[:, None, :, None] * GRID_W + key_cols[None, :, None, :]).reshape(rows, n_cb, K)
    col_ok = (key_cols[:, None, :] >= cstart[..., None]) & (key_cols[:, None, :] < cstart[..., None] + NA_WIN_W)
    valid = np.broadcast_to(col_ok[:, :, None, :], (n_cb, NA_COL_BLOCK, wr, NA_KEY_COLS)).reshape(n_cb, NA_COL_BLOCK, K)
    rel_r = key_rows - r[:, None] + NA_WIN_H - 1
    rel_c = np.clip(key_cols[:, None, :] - qcol[..., None] + NA_WIN_W - 1, 0, 2 * NA_WIN_W - 2)
    bias = rpb.astype(jnp.float32)[:, rel_r[:, None, None, :, None], rel_c[None, :, :, None, :]]
    bias = jnp.where(valid, bias.reshape(H, rows, n_cb, NA_COL_BLOCK, K), NEG_INF)

    ql = to_heads(q_lat, H, HEAD_DIM).reshape(b, H, rows, n_cb, NA_COL_BLOCK, HEAD_DIM)
    kl, vl = to_heads(k_lat, H, HEAD_DIM), to_heads(v_lat, H, HEAD_DIM)
    kc, vc = to_heads(k_ctx, H, HEAD_DIM), to_heads(v_ctx, H, HEAD_DIM)
    kg, vg = kl[:, :, key_idx], vl[:, :, key_idx]
    s_nb = jnp.einsum('bhrcqd,bhrckd->bhrcqk', ql, kg).astype(jnp.float32) * scale + bias
    s_ctx = jnp.einsum('bhrcqd,bhld->bhrcql', ql, kc).astype(jnp.float32) * scale
    p = jax.nn.softmax(jnp.concatenate([s_nb, s_ctx], axis=-1), axis=-1).astype(vl.dtype)
    o = (jnp.einsum('bhrcqk,bhrckd->bhrcqd', p[..., :K], vg)
         + jnp.einsum('bhrcql,bhld->bhrcqd', p[..., K:], vc))
    o_lat = from_heads(o.reshape(b, H, s, HEAD_DIM))
    if not with_ctx:
        return o_lat, None
    qc = to_heads(q_ctx, H, HEAD_DIM)
    pc = jax.nn.softmax(jnp.einsum('bhqd,bhld->bhql', qc, kc).astype(jnp.float32) * scale, axis=-1).astype(vc.dtype)
    return o_lat, from_heads(jnp.einsum('bhql,bhld->bhqd', pc, vc))

def qknorm_attention(q_lat, k_lat, v_lat, q_ctx, k_ctx, v_ctx, gq, gk, rope, with_ctx):
    cos, sin = rope
    b, s, _ = q_lat.shape
    L = k_ctx.shape[1]
    g = GROUP_HEADS // KV_HEADS
    nblk = s // Q_BLOCK
    scale = HEAD_DIM ** -0.5
    ql = apply_rope(rms_norm(to_heads(q_lat, GROUP_HEADS, HEAD_DIM), gq), cos, sin).reshape(b, KV_HEADS, g, s, HEAD_DIM)
    kl = apply_rope(rms_norm(to_heads(k_lat, KV_HEADS, HEAD_DIM), gk), cos, sin)
    vl = to_heads(v_lat, KV_HEADS, HEAD_DIM)
    kc = rms_norm(to_heads(k_ctx, KV_HEADS, HEAD_DIM), gk)
    vc = to_heads(v_ctx, KV_HEADS, HEAD_DIM)
    k_all = jnp.concatenate([kc, kl], axis=2)
    v_all = jnp.concatenate([vc, vl], axis=2)

    def attend(q, k, v):
        p = jax.nn.softmax(jnp.einsum('bkgqd,bksd->bkgqs', q, k).astype(jnp.float32) * scale, axis=-1)
        return jnp.einsum('bkgqs,bksd->bkgqd', p.astype(v.dtype), v)

    qb = jnp.moveaxis(ql.reshape(b, KV_HEADS, g, nblk, Q_BLOCK, HEAD_DIM), 3, 0)
    ob = lax.map(lambda qq: attend(qq, k_all, v_all), qb)
    o_lat = from_heads(jnp.moveaxis(ob, 0, 3).reshape(b, GROUP_HEADS, s, HEAD_DIM))
    if not with_ctx:
        return o_lat, None
    qc = rms_norm(to_heads(q_ctx, GROUP_HEADS, HEAD_DIM), gq).reshape(b, KV_HEADS, g, L, HEAD_DIM)
    return o_lat, from_heads(attend(qc, kc, vc).reshape(b, GROUP_HEADS, L, HEAD_DIM))

def first_inputs(seed: int = 0) -> dict:
    key = jax.random.key(seed)
    ks = jax.random.split(key, 20)
    f32 = jnp.float32
    nrm = lambda k, shape: jax.random.normal(k, shape, f32)
    return {
        'x': nrm(ks[0], (BATCH, SEQ, D_MODEL)),
        'c': nrm(ks[1], (BATCH, D_MODEL)),
        'ctx': nrm(ks[2], (BATCH, CTX_LEN, D_MODEL)),
        'c_ctx': nrm(ks[3], (D_MODEL,)),
        'w_mod': nrm(ks[4], (DEPTH, D_MODEL, 3 * D_MODEL)) * (0.5 * D_MODEL ** -0.5),
        'b_mod': nrm(ks[5], (DEPTH, 3 * D_MODEL)) * 0.02,
        'pre_norm_g': 1.0 + 0.02 * nrm(ks[6], (DEPTH, D_MODEL)),
        'w_in': nrm(ks[7], (DEPTH, D_MODEL, IN_WIDTH)) * D_MODEL ** -0.5,
        'diff_lambda_q1': nrm(ks[8], (DEPTH, DIFF_DIM)) * 0.1,
        'diff_lambda_k1': nrm(ks[9], (DEPTH, DIFF_DIM)) * 0.1,
        'diff_lambda_q2': nrm(ks[10], (DEPTH, DIFF_DIM)) * 0.1,
        'diff_lambda_k2': nrm(ks[11], (DEPTH, DIFF_DIM)) * 0.1,
        'diff_subln_g': 1.0 + 0.02 * nrm(ks[12], (DEPTH, HEAD_DIM)),
        'win_sink': nrm(ks[13], (DEPTH, GROUP_HEADS)) * 0.5,
        'na_rpb': nrm(ks[14], (DEPTH, GROUP_HEADS, 2 * NA_WIN_H - 1, 2 * NA_WIN_W - 1)) * 0.1,
        'qk_q_norm_g': 1.0 + 0.02 * nrm(ks[15], (DEPTH, HEAD_DIM)),
        'qk_k_norm_g': 1.0 + 0.02 * nrm(ks[16], (DEPTH, HEAD_DIM)),
        'w_out': nrm(ks[17], (DEPTH, MIX_WIDTH, D_MODEL)) * MIX_WIDTH ** -0.5,
        'post_norm_g': 1.0 + 0.02 * nrm(ks[18], (DEPTH, D_MODEL)),
    }

def first_block(x, c, ctx, c_ctx, w_mod, b_mod, pre_norm_g, w_in, diff_lambda_q1, diff_lambda_k1,
              diff_lambda_q2, diff_lambda_k2, diff_subln_g, win_sink, na_rpb, qk_q_norm_g, qk_k_norm_g,
              w_out, post_norm_g):
    b, s, _ = x.shape
    rope_sub = axial_rope_tables(s, DIFF_DIM, x.dtype)
    rope_head = axial_rope_tables(s, HEAD_DIM, x.dtype)
    split_points = [int(v) for v in np.cumsum(IN_SIZES)[:-1]]
    silu_c = jax.nn.silu(c)
    silu_cc = jax.nn.silu(c_ctx)
    h, hc = x, ctx
    for l in range(DEPTH):
        with_ctx = l < DEPTH - 1
        shift, scale, gate = jnp.split(silu_c @ w_mod[l] + b_mod[l], 3, axis=-1)
        shift_c, scale_c, gate_c = jnp.split(silu_cc @ w_mod[l] + b_mod[l], 3, axis=-1)
        n = rms_norm(h, pre_norm_g[l]) * (1.0 + scale[:, None]) + shift[:, None]
        nc = rms_norm(hc, pre_norm_g[l]) * (1.0 + scale_c) + shift_c
        p = jnp.split(n @ w_in[l], split_points, axis=-1)
        pc = jnp.split(nc @ w_in[l], split_points, axis=-1)

        lambda_init = 0.8 - 0.6 * math.exp(-0.3 * l)
        lam = (jnp.exp(jnp.sum(diff_lambda_q1[l].astype(jnp.float32) * diff_lambda_k1[l].astype(jnp.float32)))
               - jnp.exp(jnp.sum(diff_lambda_q2[l].astype(jnp.float32) * diff_lambda_k2[l].astype(jnp.float32)))
               + lambda_init)
        oa, oa_c = diff_attention(p[0], p[1], p[2], pc[0], pc[1], pc[2], lam, diff_subln_g[l], lambda_init,
                                  rope_sub, with_ctx)
        ob, ob_c = window_attention(p[3], p[4], p[5], pc[3], pc[4], pc[5], win_sink[l], rope_head, with_ctx)
        on, on_c = neighborhood_attention(p[6], p[7], p[8], pc[6], pc[7], pc[8], na_rpb[l], with_ctx)
        od, od_c = qknorm_attention(p[9], p[10], p[11], pc[9], pc[10], pc[11], qk_q_norm_g[l], qk_k_norm_g[l],
                                    rope_head, with_ctx)

        y = (jnp.concatenate([oa, ob, on, od], axis=-1) * jax.nn.silu(p[12])) @ w_out[l]
        h = h + gate[:, None] * rms_norm(y, post_norm_g[l])
        if with_ctx:
            yc = (jnp.concatenate([oa_c, ob_c, on_c, od_c], axis=-1) * jax.nn.silu(pc[12])) @ w_out[l]
            hc = hc + gate_c * rms_norm(yc, post_norm_g[l])
    return h


DEPTH_2 = 1

CHUNK = 64
N_META = 16

D_SSM = D_MODEL // 2
SSM_GROUP = 16
N_SSM_GROUPS = D_SSM // SSM_GROUP
SSM_STATE = 64
DT_MIN = 1e-3
DT_MAX = 1e-1

MLA_HEADS = 8
QK_NOPE = 128
QK_ROPE = 64
V_HEAD = 128
Q_LORA = 512
KV_LORA = 256
D_ATTN = MLA_HEADS * V_HEAD
ROPE_BASE = 10000.0

D_MIX = D_SSM + D_ATTN
D_IN = D_SSM + Q_LORA + KV_LORA + QK_ROPE

D_FF = 5504
CONV_W = 3


def rmsnorm(x, g):
    xf = x.astype(jnp.float32)
    y = xf * lax.rsqrt(jnp.mean(xf * xf, axis=-1, keepdims=True) + EPS)
    return (y * g.astype(jnp.float32)).astype(x.dtype)

def rotary(x, cos, sin):
    x1, x2 = jnp.split(x, 2, axis=-1)
    return jnp.concatenate([x1 * cos - x2 * sin, x2 * cos + x1 * sin], axis=-1)

def s5_mixer(u, lam_re, lam_im, log_dt, b_re, b_im, c_re, c_im, d_skip, w_glu, b_glu):
    bsz, L, _ = u.shape
    f32 = jnp.float32
    uf = u.astype(f32).reshape(bsz, L, N_SSM_GROUPS, SSM_GROUP)
    lam = lax.complex(lam_re.astype(f32), lam_im.astype(f32))
    dt = jnp.exp(log_dt.astype(f32))[:, None]
    lam_bar = jnp.exp(lam * dt)
    b = lax.complex(b_re.astype(f32), b_im.astype(f32))
    b_bar = ((lam_bar - 1.0) / lam)[..., None] * b
    bu = jnp.einsum('blgc,gpc->blgp', uf.astype(jnp.complex64), b_bar)
    a = jnp.broadcast_to(lam_bar, bu.shape)

    def combine(e1, e2):
        a1, s1 = e1
        a2, s2 = e2
        return a1 * a2, a2 * s1 + s2

    _, h = lax.associative_scan(combine, (a, bu), axis=1)
    c = lax.complex(c_re.astype(f32), c_im.astype(f32))
    y = jnp.real(jnp.einsum('blgp,gcp->blgc', h, c))
    y = y + d_skip.astype(f32).reshape(N_SSM_GROUPS, SSM_GROUP) * uf
    y = y.reshape(bsz, L, D_SSM)
    g = jax.nn.gelu(y)
    out = g * jax.nn.sigmoid(g @ w_glu.astype(f32) + b_glu.astype(f32))
    return out.astype(u.dtype)

def mla_mixer(q_a, kv_a, k_pe, q_a_norm, w_q_b, kv_a_norm, w_kv_b, cos, sin, chunk_id):
    bsz, L, _ = q_a.shape
    q = (rmsnorm(q_a, q_a_norm) @ w_q_b).reshape(bsz, L, MLA_HEADS, QK_NOPE + QK_ROPE)
    q_nope, q_pe = q[..., :QK_NOPE], q[..., QK_NOPE:]
    q_pe = rotary(q_pe, cos[:, None, :], sin[:, None, :])
    kv = (rmsnorm(kv_a, kv_a_norm) @ w_kv_b).reshape(bsz, L, MLA_HEADS, QK_NOPE + V_HEAD)
    k_nope, v = kv[..., :QK_NOPE], kv[..., QK_NOPE:]
    k_pe = rotary(k_pe, cos, sin)
    scale = 1.0 / math.sqrt(QK_NOPE + QK_ROPE)

    n_blk = -(-L // Q_BLOCK)
    pad = n_blk * Q_BLOCK - L

    def to_blocks(t):
        t = jnp.pad(t, ((0, 0), (0, pad)) + ((0, 0),) * (t.ndim - 2))
        return jnp.moveaxis(t.reshape(bsz, n_blk, Q_BLOCK, *t.shape[2:]), 1, 0)

    q_cid = jnp.pad(chunk_id, (0, pad), constant_values=2 ** 30).reshape(n_blk, Q_BLOCK)

    def attend(args):
        qn, qp, qc = args
        s = jnp.einsum('bqhd,bkhd->bhqk', qn, k_nope, preferred_element_type=jnp.float32)
        s = s + jnp.einsum('bqhr,bkr->bhqk', qp, k_pe, preferred_element_type=jnp.float32)
        mask = chunk_id[None, :] <= qc[:, None]
        s = jnp.where(mask[None, None], s * scale, jnp.finfo(jnp.float32).min)
        p = jax.nn.softmax(s, axis=-1).astype(v.dtype)
        return jnp.einsum('bhqk,bkhd->bqhd', p, v)

    o = lax.map(attend, (to_blocks(q_nope), to_blocks(q_pe), q_cid))
    o = jnp.moveaxis(o, 0, 1).reshape(bsz, n_blk * Q_BLOCK, D_ATTN)[:, :L]
    return o

def conv_ffn(x, w_up, conv_w, conv_b, w_down):
    L = x.shape[1]
    gate, val = jnp.split(x @ w_up, 2, axis=-1)
    gp = jnp.pad(gate, ((0, 0), (CONV_W - 1, 0), (0, 0)))
    gate = sum(conv_w[k] * gp[:, k:k + L] for k in range(CONV_W)) + conv_b
    return (jax.nn.silu(gate) * val) @ w_down

def second_inputs(seed: int = 0) -> dict:
    key = jax.random.key(seed)
    ks = jax.random.split(key, 32)
    f32 = jnp.float32
    nrm = lambda k, shape, s: jax.random.normal(k, shape, f32) * s
    gain = lambda k, shape: 1.0 + 0.01 * jax.random.normal(k, shape, f32)
    G, P, C = N_SSM_GROUPS, SSM_STATE, SSM_GROUP
    lam_re = -0.5 + 0.01 * jax.random.normal(ks[4], (DEPTH_2, G, P), f32)
    lam_im = jnp.pi * jnp.arange(P, dtype=f32)[None, None, :] + 0.01 * jax.random.normal(ks[5], (DEPTH_2, G, P), f32)
    log_dt = jax.random.uniform(ks[6], (DEPTH_2, G), f32, math.log(DT_MIN), math.log(DT_MAX))
    return {
        "x": jax.random.normal(ks[0], (BATCH, SEQ, D_MODEL), f32),
        "meta_tokens": nrm(ks[1], (N_META, D_MODEL), 1.0),
        "mix_norm": gain(ks[2], (DEPTH_2, D_MODEL)),
        "w_in": nrm(ks[3], (DEPTH_2, D_MODEL, D_IN), D_MODEL ** -0.5),
        "lam_re": lam_re,
        "lam_im": lam_im,
        "log_dt": log_dt,
        "b_re": nrm(ks[7], (DEPTH_2, G, P, C), (2 * C) ** -0.5),
        "b_im": nrm(ks[8], (DEPTH_2, G, P, C), (2 * C) ** -0.5),
        "c_re": nrm(ks[9], (DEPTH_2, G, C, P), (2 * P) ** -0.5),
        "c_im": nrm(ks[10], (DEPTH_2, G, C, P), (2 * P) ** -0.5),
        "d_skip": nrm(ks[11], (DEPTH_2, D_SSM), 1.0),
        "w_glu": nrm(ks[12], (DEPTH_2, D_SSM, D_SSM), D_SSM ** -0.5),
        "b_glu": nrm(ks[13], (DEPTH_2, D_SSM), 0.01),
        "q_a_norm": gain(ks[14], (DEPTH_2, Q_LORA)),
        "w_q_b": nrm(ks[15], (DEPTH_2, Q_LORA, MLA_HEADS * (QK_NOPE + QK_ROPE)), Q_LORA ** -0.5),
        "kv_a_norm": gain(ks[16], (DEPTH_2, KV_LORA)),
        "w_kv_b": nrm(ks[17], (DEPTH_2, KV_LORA, MLA_HEADS * (QK_NOPE + V_HEAD)), KV_LORA ** -0.5),
        "out_norm_ssm": gain(ks[18], (DEPTH_2, D_SSM)),
        "out_norm_attn": gain(ks[19], (DEPTH_2, D_ATTN)),
        "w_out": nrm(ks[20], (DEPTH_2, D_MIX, D_MODEL), D_MIX ** -0.5),
        "ffn_norm": gain(ks[21], (DEPTH_2, D_MODEL)),
        "w_up": nrm(ks[22], (DEPTH_2, D_MODEL, 2 * D_FF), D_MODEL ** -0.5),
        "conv_w": nrm(ks[23], (DEPTH_2, CONV_W, D_FF), CONV_W ** -0.5),
        "conv_b": nrm(ks[24], (DEPTH_2, D_FF), 0.01),
        "w_down": nrm(ks[25], (DEPTH_2, D_FF, D_MODEL), D_FF ** -0.5),
        "final_norm": gain(ks[26], (D_MODEL,)),
    }

def second_block(x, meta_tokens, mix_norm, w_in, lam_re, lam_im, log_dt, b_re, b_im, c_re, c_im,
              d_skip, w_glu, b_glu, q_a_norm, w_q_b, kv_a_norm, w_kv_b, out_norm_ssm,
              out_norm_attn, w_out, ffn_norm, w_up, conv_w, conv_b, w_down, final_norm):
    bsz = x.shape[0]
    meta = jnp.broadcast_to(meta_tokens.astype(x.dtype)[None], (bsz, N_META, D_MODEL))
    h = jnp.concatenate([meta, x], axis=1)
    L = h.shape[1]

    pos = jnp.arange(L, dtype=jnp.int32)
    chunk_id = jnp.where(pos < N_META, 0, 1 + (pos - N_META) // CHUNK)
    inv_freq = 1.0 / (ROPE_BASE ** (jnp.arange(0, QK_ROPE, 2, dtype=jnp.float32) / QK_ROPE))
    ang = pos.astype(jnp.float32)[:, None] * inv_freq[None, :]
    cos = jnp.cos(ang).astype(x.dtype)
    sin = jnp.sin(ang).astype(x.dtype)

    for i in range(DEPTH_2):
        xn = rmsnorm(h, mix_norm[i])
        z = xn @ w_in[i]
        o1 = D_SSM
        o2 = o1 + Q_LORA
        o3 = o2 + KV_LORA
        u, q_a, kv_a, k_pe = z[..., :o1], z[..., o1:o2], z[..., o2:o3], z[..., o3:]
        ya = s5_mixer(u, lam_re[i], lam_im[i], log_dt[i], b_re[i], b_im[i], c_re[i], c_im[i],
                      d_skip[i], w_glu[i], b_glu[i])
        yb = mla_mixer(q_a, kv_a, k_pe, q_a_norm[i], w_q_b[i], kv_a_norm[i], w_kv_b[i],
                       cos, sin, chunk_id)
        y = jnp.concatenate([rmsnorm(ya, out_norm_ssm[i]), rmsnorm(yb, out_norm_attn[i])], axis=-1)
        h = h + y @ w_out[i]
        h = h + conv_ffn(rmsnorm(h, ffn_norm[i]), w_up[i], conv_w[i], conv_b[i], w_down[i])

    return rmsnorm(h, final_norm)[:, N_META:]


_first_inputs = second_inputs


def second_inputs(seed=0):
    import zlib

    import numpy as np

    out = dict(_first_inputs(seed))
    spreads = {}
    factors = {'mix_norm': 5.232,
     'lam_re': 64.0,
     'b_glu': 25.292,
     'q_a_norm': 8.0,
     'kv_a_norm': 7.081,
     'out_norm_ssm': 45.964,
     'out_norm_attn': 45.764,
     'ffn_norm': 31.393,
     'conv_b': 45.484,
     'final_norm': 33.567,
     'b_re': 2.679,
     'c_re': 2.686,
     'c_im': 2.691}
    for name, (base, spread) in spreads.items():
        noise = np.random.default_rng([zlib.crc32(name.encode()), seed]).standard_normal(out[name].shape)
        drawn = base * np.exp(spread * noise) if base else spread * noise
        out[name] = __import__('jax').numpy.asarray(drawn.astype(out[name].dtype))
    for name, factor in factors.items():
        out[name] = (out[name] * factor).astype(out[name].dtype)
    return out


_narrow_inputs = second_inputs


def second_inputs(seed=0):

    out = dict(_narrow_inputs(seed))
    wider = {'lam_re': 12.0,
     'b_im': 3.11,
     'out_norm_ssm': 6.35,
     'out_norm_attn': 6.38,
     'ffn_norm': 4.37,
     'conv_b': 4.37,
     'final_norm': 6.52}
    for name, times in wider.items():
        mean = out[name].mean()
        out[name] = (mean + times * (out[name] - mean)).astype(out[name].dtype)
    return out


def setup_inputs(seed=0):
    out = dict(first_inputs(seed))
    for name, value in second_inputs(seed + 1).items():
        if name != "x":
            out[name + "_2"] = value
    return out


def reference(
    x, c, ctx, c_ctx, w_mod, b_mod, pre_norm_g, w_in, diff_lambda_q1, diff_lambda_k1,
    diff_lambda_q2, diff_lambda_k2, diff_subln_g, win_sink, na_rpb, qk_q_norm_g, qk_k_norm_g,
    w_out, post_norm_g, meta_tokens_2, mix_norm_2, w_in_2, lam_re_2, lam_im_2, log_dt_2, b_re_2,
    b_im_2, c_re_2, c_im_2, d_skip_2, w_glu_2, b_glu_2, q_a_norm_2, w_q_b_2, kv_a_norm_2,
    w_kv_b_2, out_norm_ssm_2, out_norm_attn_2, w_out_2, ffn_norm_2, w_up_2, conv_w_2, conv_b_2,
    w_down_2, final_norm_2,
):
    x = first_block(
        x, c, ctx, c_ctx, w_mod, b_mod, pre_norm_g, w_in, diff_lambda_q1, diff_lambda_k1,
        diff_lambda_q2, diff_lambda_k2, diff_subln_g, win_sink, na_rpb, qk_q_norm_g,
        qk_k_norm_g, w_out, post_norm_g,
    )
    return second_block(
        x, meta_tokens_2, mix_norm_2, w_in_2, lam_re_2, lam_im_2, log_dt_2, b_re_2, b_im_2,
        c_re_2, c_im_2, d_skip_2, w_glu_2, b_glu_2, q_a_norm_2, w_q_b_2, kv_a_norm_2, w_kv_b_2,
        out_norm_ssm_2, out_norm_attn_2, w_out_2, ffn_norm_2, w_up_2, conv_w_2, conv_b_2,
        w_down_2, final_norm_2,
    )


_drawn_inputs = setup_inputs


def setup_inputs(seed=0):
    import zlib

    import numpy as np

    out = dict(_drawn_inputs(seed))
    spreads = {}
    factors = {'win_sink': 8.0,
     'qk_q_norm_g': 8.0,
     'qk_k_norm_g': 6.682,
     'lam_re_2': 162.552,
     'lam_im_2': 23.048,
     'log_dt_2': 21.616,
     'b_re_2': 8.0,
     'b_im_2': 8.0,
     'c_re_2': 8.0,
     'c_im_2': 8.0}
    for name, (base, spread) in spreads.items():
        noise = np.random.default_rng([zlib.crc32(name.encode()), seed]).standard_normal(out[name].shape)
        drawn = base * np.exp(spread * noise) if base else spread * noise
        out[name] = __import__('jax').numpy.asarray(drawn.astype(out[name].dtype))
    for name, factor in factors.items():
        out[name] = (out[name] * factor).astype(out[name].dtype)
    return out
```

```python
import math

import numpy as np

import concourse.bass as bass
from concourse import mybir

F32 = mybir.dt.float32
ALU = mybir.AluOpType
ACT = mybir.ActivationFunctionType
AX = mybir.AxisListType

P = 128
D = 2048
KT = D // P
DEPTH = 2
LAT, CTX = 256, 256
NT = (LAT + CTX) // P
LT = LAT // P
GRID = 64
HD = 128
HEADS = 4
SUB = 64
CH = 512
MODC = 3 * D // CH
INC = 14
EPS = 1e-6
MASKED = -1e30
PIECE = 2048
RING = 5

META = 16
T2 = META + LAT
Q0 = META - 2
TQ = T2 - Q0
DS = 1024
ST = DS // P
SJ = 32
MH = 8
QL, KL = 512, 256
FF = 5504
FT = FF // P
CONVW = 3
HALF_UP = 12582912.0
TWO_PI = 6.283185

VEC = {}


def _columns():
    at = 0
    for name, n in (("pre_g", 2 * KT), ("post_g", 2 * KT), ("b_mod", 2 * 3 * KT), ("sink", 2 * HEADS),
                    ("silu_in", 2 * KT), ("lambda_in", 2 * 4 * SUB),
                    ("mix_g", KT), ("ffn_g", KT), ("b_glu", ST), ("d_skip", ST), ("qa_g", QL // P), ("kva_g", KL // P),
                    ("ssm_g", ST), ("attn_g", ST), ("conv_w", CONVW * FT), ("conv_b", FT),
                    ("lam_re", SJ), ("lam_im", SJ), ("log_dt", SJ)):
        VEC[name] = (at, at + n)
        at += n
    return at


NVEC = _columns()

CONST = {}


def _constants(*entries):
    at = 0
    for name, n in entries:
        CONST[name] = (at, at + n)
        at += n
    return at


NCONST = _constants(("ident", P), ("ones", P), ("minus_half", 1))
NCONST1 = _constants(("cos_h", LT * SUB), ("sin_h", LT * SUB), ("cos_s", LT * 32), ("sin_s", LT * 32),
                     ("win_mask", LT * LAT), ("na_mask", LT * LAT))
NCONST2 = _constants(("mla_mask", LT * T2), ("pe_turn", P), ("pe_pair", P), ("pe_turn_pair", P), ("pe_cos", T2),
                     ("pe_sin", T2), ("steps", T2))
FIRST_ONLY = ("cos_h", "sin_h", "cos_s", "sin_s", "win_mask", "na_mask")
BOTH = ("ident", "ones", "minus_half")



class Queue:

    def __init__(self, sem):
        self.sem, self.count, self.todo, self.seen = sem, 0, [], {}

    def wait(self, *points):
        for point in points:
            if point is None:
                continue
            sem, count = point
            if self.seen.get(sem.name, 0) < count:
                self.seen[sem.name] = count
                self.todo.append(lambda e, s=sem, c=count: e.wait_ge(s, c))

    def do(self, make, *points, mark=True):
        self.wait(*points)
        if not mark:
            self.todo.append(make)
            return None
        self.count += 1
        self.todo.append(lambda e, s=self.sem: make(e).then_inc(s, 1))
        return (self.sem, self.count)

    def last(self):
        return (self.sem, self.count)

    def emit(self, engine):
        for make in self.todo:
            make(engine)


class Load:

    def __init__(self, sem):
        self.sem, self.count = sem, 0

    def start(self, queue, dst, src, *points):
        queue.wait(*points)
        self.count += 16
        queue.todo.append(lambda e, s=self.sem: e.dma_start(dst, src).then_inc(s, 16))
        return (self.sem, self.count)


class Bank:

    def __init__(self, tensor):
        self.t, self.free = tensor, None

    def __getitem__(self, key):
        return self.t[key]


def bc(ap, axis, shape):
    return ap.unsqueeze(axis).broadcast_to(shape)


def build(nc, A, out):
    names = {}

    def sem(name):
        s = nc.semaphore(name)
        names[name] = s
        return s.__enter__()

    V, S, G, T, Y = (Queue(sem(n)) for n in ("vector_done", "scalar_done", "gpsimd_done", "tensor_done", "sync_done"))

    arena_words = 53200
    arena = nc.sbuf_tensor("arena", [P, arena_words], F32).__enter__()
    banks = [Bank(nc.psum_tensor(f"bank{i}", [P, CH], F32).__enter__()) for i in range(8)]
    top = [0]

    def room(words):
        at = top[0]
        top[0] += words
        assert top[0] <= arena_words, top[0]
        return arena[:, at:at + words]

    def room3(a, b):
        return room(a * b).rearrange("p (a b) -> p a b", b=b)

    slots = room3(RING, PIECE)
    consts = room(NCONST)
    block_consts = [None]
    vecs = room(NVEC)

    def const(name):
        return (consts if name in BOTH else block_consts[0])[:, CONST[name][0]:CONST[name][1]]

    def vec(name):
        return vecs[:, VEC[name][0]:VEC[name][1]]

    def col(name, i):
        return vecs[:, VEC[name][0] + i:VEC[name][0] + i + 1]

    ident, ones = const("ident"), const("ones")
    mod_cols = room3(3 * KT, 2)
    scaled_g = room3(KT, 2)
    small = room(256)
    small_at = [0]

    def cols(n):
        at = small_at[0]
        small_at[0] += n
        assert small_at[0] <= 256
        return small[:, at:at + n]

    slot_loads = [Load(sem(f"slot{i}_loaded")) for i in range(RING)]
    slot_free = [None] * RING
    piece_no = [0]

    def piece(src, words=PIECE):
        i = piece_no[0] % RING
        piece_no[0] += 1
        here = slot_loads[i].start(Y, slots[:, i, 0:words], src, slot_free[i])
        return slots[:, i, 0:words], here, i

    turned = []
    side_work = []
    clock = [0]

    def side(n=1):
        for _ in range(n):
            clock[0] += 1
            if turned:
                if turned[0][0] < clock[0]:
                    turned.pop(0)[1]()
            elif side_work:
                try:
                    next(side_work[0])
                except StopIteration:
                    side_work.pop(0)

    def side_all():
        while turned or side_work:
            side()

    flip = [0]

    def copy_out(dst, src, *points):
        flip[0] ^= 1
        if flip[0]:
            return S.do(lambda e: e.activation(dst, src, ACT.Copy), *points)
        return V.do(lambda e: e.tensor_copy(dst, src), *points)

    load_c, load_v, load_x = Load(sem("consts_loaded")), Load(sem("vectors_loaded")), Load(sem("x_loaded"))
    load_ctx, load_bias = Load(sem("ctx_loaded")), Load(sem("bias_loaded"))
    have_v = load_v.start(S, vecs, A["vectors"])
    have_c = load_c.start(S, consts, A["consts"])
    common_top = top[0]
    block_consts[0] = room(NCONST1)
    have_c = load_c.start(S, block_consts[0], A["consts_1"])
    for q in (V, G, T):
        q.wait(have_v, have_c)
    S.wait(have_v, have_c)

    hid = room3(NT, D)
    feat = room3(KT, NT * P)
    h_lat = room3(LT, D)
    pairs = []
    pairs_at = top[0]
    for kvh in (HEADS, 2):
        pairs.append((room3(HEADS, NT * P), room3(kvh, NT * P), room3(NT, kvh * HD)))
    ctx_old = arena[:, pairs_at:pairs_at + LT * D].rearrange("p (a b) -> p a b", b=D)
    probs = [[room(CH), room(CH)] for _ in range(2)]
    probs_t = [room(CH) for _ in range(2)]
    turn_a = room(CH)
    turn_b = room(CH)
    rows_buf = [room(CH) for _ in range(2)]
    scratch = room(CH)
    na_bias = room3(HEADS * LT, LAT)
    mod_rows = scratch
    print("first block words", top[0])

    subln = room(P)
    qk_g = room3(2, HD)

    ssq = cols(NT * 4)
    rstd = cols(NT)
    lam_col, lam_t = cols(1), cols(4)
    mx = [cols(4) for _ in range(4)]
    sums = [cols(HEADS) for _ in range(2)]
    rinv = [cols(HEADS) for _ in range(2)]
    dif = [cols(4) for _ in range(2)]
    hss = cols(HEADS * 2)
    silu_c = room3(KT, 2)

    have_x = load_x.start(S, h_lat, A["x"])
    have_ctx = load_ctx.start(S, hid[:, 2:4, :], A["ctx"])

    c_in = vec("silu_in").rearrange("p (k s) -> p k s", s=2)
    p = S.do(lambda e: e.activation(silu_c, c_in, ACT.Tanh, scale=0.5))
    p = V.do(lambda e: e.scalar_tensor_tensor(out=silu_c, in0=silu_c, scalar=1.0, in1=c_in, op0=ALU.add, op1=ALU.mult), p)
    silu_ready = V.do(lambda e: e.tensor_scalar(silu_c, silu_c, 0.5, None, ALU.mult), p)

    state = {"small": silu_ready, "feat": None, "hid_lat": None, "scratch": None, "mod": None}
    acc_turn = [0]

    def next_acc():
        acc_turn[0] = (acc_turn[0] + 1) % 3
        return banks[acc_turn[0]]

    def modulation(l):
        for c in range(MODC):
            bank = next_acc()
            for kg in range(4):
                w, here, i = piece(A["w_mod"][l, c, kg])
                for k in range(4):
                    done = T.do(lambda e, w=w, k=k, kg=kg, bank=bank: e.matmul(
                        bank[0:2, :], silu_c[:, 4 * kg + k, :], w[:, k * CH:(k + 1) * CH],
                        start=kg + k == 0, stop=kg + k == 6),
                        here, silu_ready, bank.free, mark=k == 3)
                slot_free[i] = done
                side()
            r = mod_rows[0:2, :]
            bank.free = V.do(lambda e, b=bank: e.tensor_copy(r, b[0:2, :]), done, state["scratch"])
            tb = banks[5 + c % 2]
            for j in range(4):
                t = T.do(lambda e, j=j, tb=tb: e.transpose(tb[:, 2 * j:2 * j + 2], r[:, j * P:(j + 1) * P],
                                                          ident[0:2, 0:2]), bank.free, tb.free, mark=j == 3)
            state["scratch"] = t
            b0 = VEC["b_mod"][0] + l * 3 * KT + 4 * c
            tb.free = V.do(lambda e, tb=tb, c=c, b0=b0: e.tensor_tensor(
                mod_cols[:, 4 * c:4 * c + 4, :], tb[:, 0:8].rearrange("p (j s) -> p j s", s=2),
                bc(vecs[:, b0:b0 + 4], 2, (P, 4, 2)), ALU.add), t, state["mod"])
        gate = mod_cols[:, 2 * KT:, :]
        state["gate_ready"] = V.do(lambda e: e.tensor_tensor(gate, gate, bc(vec("post_g")[:, l * KT:(l + 1) * KT], 2, (P, KT, 2)),
                                                             ALU.mult), tb.free)
        p1 = V.do(lambda e: e.tensor_scalar(scaled_g, mod_cols[:, KT:2 * KT, :], 1.0, None, ALU.add), tb.free, state["mod"])
        g0 = VEC["pre_g"][0] + l * KT
        state["mod_ready"] = V.do(lambda e: e.tensor_tensor(scaled_g, scaled_g, bc(vecs[:, g0:g0 + KT], 2, (P, KT, 2)),
                                                            ALU.mult), p1)

    load_subln = Load(sem("gains_loaded"))

    def layer_consts(l):
        before = state.get("consts_free", ())
        state["gains"] = load_subln.start(S, subln, A["subln"][l], *before)
        state["gains"] = load_subln.start(S, qk_g, A["qk_g"][l])
        have = load_bias.start(S, na_bias, A["na_bias"][l])
        m = const("na_mask").rearrange("p (t k) -> p t k", k=LAT)
        p1 = None
        for h in range(HEADS):
            b = na_bias[:, h * LT:(h + 1) * LT, :]
            p1 = G.do(lambda e, b=b: e.tensor_tensor(b, b, m, ALU.add), have)
        state["na_ready"] = p1
        lv = vec("lambda_in").rearrange("p (l v d) -> p l v d", v=4, d=SUB)[:, l]
        prod = turn_a[:, 0:2 * SUB].rearrange("p (v d) -> p v d", d=SUB)
        p2 = V.do(lambda e: e.tensor_tensor(prod, lv[:, 0:3:2, :], lv[:, 1:4:2, :], ALU.mult), state.get("turn_free"))
        p2 = V.do(lambda e: e.tensor_reduce(lam_t[:, 0:2], prod, AX.X, ALU.add), p2)
        p2 = S.do(lambda e: e.activation(lam_t[:, 2:4], lam_t[:, 0:2], ACT.Exp), p2)
        p2 = V.do(lambda e: e.tensor_tensor(lam_col, lam_t[:, 2:3], lam_t[:, 3:4], ALU.subtract), p2)
        lam_init = 0.8 - 0.6 * math.exp(-0.3 * l)
        state["lam"] = V.do(lambda e: e.tensor_scalar(lam_col, lam_col, lam_init, None, ALU.add), p2)
        state["turn_free"] = p2

    def power(dst, *points, words=None):
        n = dst.shape[-1]
        mh = const("minus_half")[0:dst.shape[0], :].broadcast_to((dst.shape[0], n))
        return G.do(lambda e: e.tensor_tensor(dst, dst, mh, ALU.pow), *points)

    def pre_norm(l):
        scaled = [None] * NT
        for t in range(NT):
            src = h_lat[:, t, :] if t < LT else hid[:, t, :]
            have = state["h"][t]
            for c in range(4):
                p1 = S.do(lambda e, c=c, src=src, t=t: e.activation(
                    scratch, src[:, c * CH:(c + 1) * CH], ACT.Square, accum_out=ssq[:, 4 * t + c:4 * t + c + 1]),
                    have, state["scratch"])
                state["scratch"] = p1
            p1 = V.do(lambda e, t=t: e.tensor_reduce(rstd[:, t:t + 1], ssq[:, 4 * t:4 * t + 4], AX.X, ALU.add), p1)
            p1 = V.do(lambda e, t=t: e.tensor_scalar(rstd[:, t:t + 1], rstd[:, t:t + 1], 1.0 / D, EPS, ALU.mult, ALU.add), p1)
            p1 = power(rstd[:, t:t + 1], p1)
            scaled[t] = V.do(lambda e, t=t, src=src: e.tensor_scalar(hid[:, t, :], src, rstd[:, t:t + 1], None, ALU.mult),
                             p1, have)
        done = []
        for f in range(KT):
            tb = banks[5 + f % 2] if f % 4 < 2 else banks[3 + f % 2]
            for t in range(NT):
                p1 = T.do(lambda e, f=f, t=t, tb=tb: e.transpose(tb[:, t * P:(t + 1) * P], hid[:, t, f * P:(f + 1) * P], ident),
                          scaled[t], tb.free, mark=t == NT - 1)
            for s in range(2):
                o = feat[:, f, s * LAT:(s + 1) * LAT]
                i = tb[:, s * LAT:(s + 1) * LAT]
                g, b = scaled_g[:, f, s:s + 1], mod_cols[:, f, s:s + 1]
                if f % 2:
                    tb.free = S.do(lambda e, o=o, i=i, g=g, b=b: e.activation(o, i, ACT.Identity, scale=g, bias=b),
                                   p1, state["mod_ready"], state["feat"])
                else:
                    tb.free = V.do(lambda e, o=o, i=i, g=g, b=b: e.tensor_scalar(o, i, g, b, ALU.mult, ALU.add),
                                   p1, state["mod_ready"], state["feat"])
            done.append(tb.free)
        state["feat_ready"] = done
        state["mod"] = done[-2]
        state["mod_s"] = done[-1]
        state["hid_free"] = p1

    def project(src_piece, tiles, finish):
        ws = [piece(src_piece[kg]) for kg in range(4)]
        for n, t in enumerate(tiles):
            bank = next_acc()
            for kg in range(4):
                w, here, i = ws[kg]
                for k in range(4):
                    kk = 4 * kg + k
                    done = T.do(lambda e, w=w, k=k, kk=kk, bank=bank, t=t: e.matmul(
                        bank[:, :], feat[:, kk, t * P:(t + 1) * P], w[:, k * CH:(k + 1) * CH],
                        start=kk == 0, stop=kk == KT - 1),
                        here, bank.free, state["feat_ready"][kk], mark=k == 3)
                if n == len(tiles) - 1:
                    slot_free[i] = done
                side()
            finish(t, bank, done)

    row_turn = [0]
    rows_free = [None, None]
    head_ready = {}
    group_free = [(), ()]

    def rotate(x, r, t, nh, sub, points):
        half = (SUB if sub else HD) // 2
        n = nh * 2 if sub else nh
        cs = const("cos_s" if sub else "cos_h")[:, t * half:(t + 1) * half]
        sn = const("sin_s" if sub else "sin_h")[:, t * half:(t + 1) * half]
        w = nh * HD

        def v4(ap):
            return ap.rearrange("p (n s d) -> p n s d", s=2, d=half)
        cosb = cs.unsqueeze(1).unsqueeze(1).broadcast_to((P, n, 2, half))
        sinb = bc(sn, 1, (P, n, half))
        a, b = turn_a[:, 0:w], turn_b[:, 0:w]
        p1 = V.do(lambda e: e.tensor_tensor(v4(a), v4(x), cosb, ALU.mult), *points, state.get("turn_free"), state.get("turn_free2"))
        p2 = V.do(lambda e: e.tensor_tensor(v4(b)[:, :, 0, :], v4(x)[:, :, 1, :], sinb, ALU.mult), *points)
        p3 = V.do(lambda e: e.tensor_tensor(v4(b)[:, :, 1, :], v4(x)[:, :, 0, :], sinb, ALU.mult), *points)
        p4 = G.do(lambda e: e.tensor_tensor(v4(r)[:, :, 0, :], v4(a)[:, :, 0, :], v4(b)[:, :, 0, :], ALU.subtract), p1, p3)
        p5 = G.do(lambda e: e.tensor_tensor(v4(r)[:, :, 1, :], v4(a)[:, :, 1, :], v4(b)[:, :, 1, :], ALU.add), p1, p3)
        state["turn_free"] = p5
        return p3, p5

    def finish_heads(kind, x_cut, nh, dst, gain, key, parity):
        def finish(t, bank, done):
            x = bank[:, x_cut]
            b = row_turn[0] % 2
            row_turn[0] += 1
            w = nh * HD
            r = rows_buf[b][:, 0:w]
            points = (done, rows_free[b])
            if gain is not None:
                def h3(ap):
                    return ap.rearrange("p (h d) -> p h d", d=HD)
                hs = hss[:, 0:nh]
                p1 = S.do(lambda e: e.activation(turn_a[:, 0:w], x, ACT.Square), done, state.get("turn_free"), state.get("turn_free2"))
                p1 = V.do(lambda e: e.tensor_reduce(hs, h3(turn_a[:, 0:w]), AX.X, ALU.add), p1)
                p1 = V.do(lambda e: e.tensor_scalar(hs, hs, 1.0 / HD, EPS, ALU.mult, ALU.add), p1)
                p1 = power(hs, p1)
                p2 = V.do(lambda e: e.tensor_tensor(h3(scratch[:, 0:w]), h3(x), bc(hs, 2, (P, nh, HD)), ALU.mult),
                          p1, done, state["scratch"])
                bank.free = p2
                y = r if t >= LT else scratch[:, 0:w]
                p3 = V.do(lambda e: e.tensor_tensor(h3(y), h3(scratch[:, 0:w]), bc(qk_g[:, gain, :], 1, (P, nh, HD)), ALU.mult),
                          p2, state["gains"], rows_free[b])
                state["scratch"] = p3
                state["turn_free2"] = p2
                if t < LT:
                    read, ready = rotate(y, r, t, nh, False, (p3, rows_free[b]))
                    state["scratch"] = read
                else:
                    ready = p3
                extra = p3
            elif t < LT and kind in ("sub", "head"):
                bank.free, ready = rotate(x, r, t, nh, kind == "sub", points)
                G.wait(rows_free[b])
            else:
                ready = bank.free = S.do(lambda e: e.activation(r, x, ACT.Copy), *points)

            def turn():
                tb = banks[5 + b]
                for h in range(nh):
                    p1 = T.do(lambda e, h=h: e.transpose(tb[:, h * P:(h + 1) * P], r[:, h * P:(h + 1) * P], ident),
                              ready, tb.free, mark=h == nh - 1)
                rows_free[b] = p1
                tb.free = S.do(lambda e: e.activation(dst[:, 0:nh, t * P:(t + 1) * P],
                                                      tb[:, 0:w].rearrange("p (h q) -> p h q", q=P), ACT.Copy),
                               p1, *group_free[parity])
                head_ready[(*key, t)] = tb.free
            turned.append((clock[0] + 1, turn))
        return finish

    def finish_v(x_cut, w, v, key, parity, then=None):
        def finish(t, bank, done):
            p1 = V.do(lambda e: e.tensor_copy(v[:, t, 0:w], bank[:, x_cut]), done, *group_free[parity])
            head_ready[(*key, t)] = p1
            bank.free = p1
            if then is not None:
                then(t, bank, p1)
        return finish

    unit_no = [0]
    probs_free = [None, None]
    exp_done = [None] * 4
    probs_t_free = [None, None]
    out_turn = [0]
    last_read = {}
    attended = set()

    def attention(l, g, kind, kv_heads, q, k, v, tiles, parity):
        scale = (SUB if kind == "diff" else HD) ** -0.5
        lam_init = 0.8 - 0.6 * math.exp(-0.3 * l)
        obank = banks[7]
        units = [(t, h) for t in tiles for h in range(HEADS)]
        work = {}

        def scores(t, h):
            u = unit_no[0] % 2
            m = mx[unit_no[0] % 4]
            older = exp_done[unit_no[0] % 4]
            k0 = 0 if t < LT else LAT
            n = NT * P - k0
            hk = h // (HEADS // kv_heads)
            keys = tuple(head_ready[(g, "k", tt)] for tt in range(k0 // P, NT))
            pa, pb = probs[u][0][:, 0:n], probs[u][1][:, 0:n]
            sm = sums[t % 2]
            if kind == "diff":
                dd = dif[u]
                es = []
                for s in range(2):
                    sb = banks[3 + s]
                    p1 = T.do(lambda e, s=s, sb=sb: e.matmul(
                        sb[:, 0:n], q[s * SUB:(s + 1) * SUB, h, t * P:(t + 1) * P], k[s * SUB:(s + 1) * SUB, hk, k0:NT * P],
                        start=True, stop=True), head_ready[(g, "q", t)], *keys, sb.free)
                    p2 = V.do(lambda e, s=s, sb=sb: e.tensor_reduce(m[:, s:s + 1], sb[:, 0:n], AX.X, ALU.max), p1, older)
                    p2 = V.do(lambda e, s=s: e.tensor_scalar(m[:, s:s + 1], m[:, s:s + 1], -scale, None, ALU.mult), p2)
                    o = (pa, pb)[s]
                    sb.free = S.do(lambda e, s=s, sb=sb, o=o: e.activation(
                        o, sb[:, 0:n], ACT.Exp, bias=m[:, s:s + 1], scale=scale, accum_out=dd[:, s:s + 1]),
                        p2, probs_free[u])
                    es.append(sb.free)
                p3 = V.do(lambda e: e.reciprocal(dd[:, 2:4], dd[:, 0:2]), es[1])
                p4 = V.do(lambda e: e.tensor_scalar(dd[:, 3:4], dd[:, 3:4], lam_col, None, ALU.mult), p3, state["lam"])
                p4 = V.do(lambda e: e.tensor_scalar(pb, pb, dd[:, 3:4], None, ALU.mult), p4)
                p4 = V.do(lambda e: e.scalar_tensor_tensor(out=pa, in0=pa, scalar=dd[:, 2:3], in1=pb,
                                                           op0=ALU.mult, op1=ALU.subtract), p4)
                exp_done[unit_no[0] % 4] = es[1]
                work[(t, h)] = (u, pa, p4, k0)
            else:
                sb = banks[3 + u]
                p1 = T.do(lambda e: e.matmul(sb[:, 0:n], q[:, h, t * P:(t + 1) * P], k[:, hk, k0:NT * P],
                                             start=True, stop=True), head_ready[(g, "q", t)], *keys, sb.free)
                src, sc, points = sb[:, 0:n], scale, (p1,)
                biased = t < LT and kind in ("win", "na")
                if biased:
                    bias = (const("win_mask")[:, t * LAT:(t + 1) * LAT] if kind == "win" else na_bias[:, h * LT + t, :])
                    p2 = V.do(lambda e: e.scalar_tensor_tensor(out=pb[:, 0:LAT], in0=sb[:, 0:LAT], scalar=scale, in1=bias,
                                                               op0=ALU.mult, op1=ALU.add),
                              p1, probs_free[u], state["na_ready"], exp_done[(unit_no[0] - 2) % 4])
                    sb.free = S.do(lambda e: e.activation(pb[:, LAT:], sb[:, LAT:n], ACT.Copy, scale=scale), p2)
                    src, sc, points = pb, 1.0, (sb.free,)
                p2 = V.do(lambda e: e.tensor_reduce(m[:, 0:1], src, AX.X, ALU.max), *points, older)
                if kind == "win":
                    sink = col("sink", l * HEADS + h)
                    p2 = V.do(lambda e: e.tensor_scalar(m[:, 0:1], m[:, 0:1], sc, sink, ALU.mult, ALU.max), p2)
                    p2 = V.do(lambda e: e.tensor_scalar(m[:, 0:1], m[:, 0:1], -1.0, None, ALU.mult), p2)
                else:
                    p2 = V.do(lambda e: e.tensor_scalar(m[:, 0:1], m[:, 0:1], -sc, None, ALU.mult), p2)
                p3 = S.do(lambda e: e.activation(pa, src, ACT.Exp, bias=m[:, 0:1], scale=sc, accum_out=sm[:, h:h + 1]),
                          p2, probs_free[u], last_read.get(("sums", t % 2)))
                if not biased:
                    sb.free = p3
                summed = p3
                if kind == "win":
                    p4 = S.do(lambda e: e.activation(m[:, 1:2], sink, ACT.Exp, bias=m[:, 0:1]), p2)
                    summed = V.do(lambda e: e.tensor_tensor(sm[:, h:h + 1], sm[:, h:h + 1], m[:, 1:2], ALU.add), p4, p3)
                exp_done[unit_no[0] % 4] = summed if kind != "win" else p4
                last_read[("summed", t % 2)] = summed
                work[(t, h)] = (u, pa, p3, k0)
            unit_no[0] += 1

        def flip_probs(t, h):
            u, pa, ready, k0 = work[(t, h)]
            nk = NT - k0 // P
            tb = banks[5 + u]
            for j in range(nk):
                p1 = T.do(lambda e, j=j: e.transpose(tb[:, j * P:(j + 1) * P], pa[:, j * P:(j + 1) * P], ident),
                          ready, tb.free, mark=j == nk - 1)
            probs_free[u] = p1
            tb.free = copy_out(probs_t[u][:, 0:nk * P], tb[:, 0:nk * P], p1, probs_t_free[u])
            work[(t, h)] = (u, tb.free, k0)

        def values(t, h):
            u, ready, k0 = work[(t, h)]
            nk = NT - k0 // P
            hk = h // (HEADS // kv_heads)
            for j in range(nk):
                kt = k0 // P + j
                p1 = T.do(lambda e, j=j, kt=kt: e.matmul(obank[:, h * HD:(h + 1) * HD], probs_t[u][:, j * P:(j + 1) * P],
                                                         v[:, kt, hk * HD:(hk + 1) * HD], start=j == 0, stop=j == nk - 1),
                          ready, obank.free, head_ready[(g, "v", kt)], mark=j == nk - 1)
            probs_t_free[u] = p1
            if h < HEADS - 1:
                return
            dst = hid[:, t, g * CH:(g + 1) * CH]

            def h3(ap):
                return ap.rearrange("p (h d) -> p h d", d=HD)
            if kind == "diff":
                hs = hss[:, HEADS:2 * HEADS]
                p2 = S.do(lambda e: e.activation(dst, obank[:, :], ACT.Square), p1, state["hid_free"])
                p2 = V.do(lambda e: e.tensor_reduce(hs, h3(dst), AX.X, ALU.add), p2)
                p2 = V.do(lambda e: e.tensor_scalar(hs, hs, 1.0 / HD, EPS, ALU.mult, ALU.add), p2)
                p2 = power(hs, p2)
                p2 = V.do(lambda e: e.tensor_tensor(h3(dst), h3(obank[:, :]), bc(hs, 2, (P, HEADS, HD)), ALU.mult), p2)
                obank.free = p2
                p2 = V.do(lambda e: e.scalar_tensor_tensor(out=h3(dst), in0=h3(dst), scalar=1.0 - lam_init,
                                                           in1=bc(subln, 1, (P, HEADS, HD)), op0=ALU.mult, op1=ALU.mult),
                          p2, state["gains"])
            else:
                ri = rinv[t % 2]
                p2 = V.do(lambda e: e.reciprocal(ri, sums[t % 2]), last_read[("summed", t % 2)])
                last_read[("sums", t % 2)] = p2
                p2 = V.do(lambda e: e.tensor_tensor(h3(dst), h3(obank[:, :]), bc(ri, 2, (P, HEADS, HD)), ALU.mult),
                          p2, p1, state["hid_free"])
                obank.free = p2
            head_ready[(g, "o", t)] = p2

        for i in range(len(units) + 2):
            if i < len(units):
                scores(*units[i])
            if 0 <= i - 1 < len(units):
                flip_probs(*units[i - 1])
            if 0 <= i - 2 < len(units):
                values(*units[i - 2])
            yield
        group_free[parity] = (T.last(),)
        attended.add(g)

    def finish_gate(g):
        def finish(t, bank, done):
            u = row_turn[0] % 2
            row_turn[0] += 1
            r = rows_buf[u]
            dst = hid[:, t, g * CH:(g + 1) * CH]
            p1 = S.do(lambda e: e.activation(r, bank[:, :], ACT.Tanh, scale=0.5), done, rows_free[u])
            p2 = V.do(lambda e: e.scalar_tensor_tensor(out=r, in0=r, scalar=1.0, in1=bank[:, :], op0=ALU.add, op1=ALU.mult), p1)
            bank.free = p2
            p3 = V.do(lambda e: e.scalar_tensor_tensor(out=dst, in0=r, scalar=0.5, in1=dst, op0=ALU.mult, op1=ALU.mult),
                      p2, head_ready[(g, "o", t)])
            rows_free[u] = p3
            head_ready[(g, "mix", t)] = p3
        return finish

    def layer(l):
        tiles = list(range(NT))
        qtiles = tiles if l < DEPTH - 1 else tiles[:LT]
        w = A["w_in"]
        plan = [("diff", HEADS, 0, ("q", "k", "v")), ("win", 2, 3, ("q", "kv")),
                ("na", HEADS, 5, ("q", "k", "v")), ("qk", 2, 8, ("q", "kv"))]
        rope = {"diff": "sub", "win": "head", "na": None, "qk": "head"}
        full = slice(0, CH)
        attended.clear()
        for g, (kind, kvh, c0, parts) in enumerate(plan):
            parity = g % 2
            while g >= 2 and g - 2 not in attended:
                side()
            q, k, v = pairs[parity]
            gq, gk = (0, 1) if kind == "qk" else (None, None)
            for n, part in enumerate(parts):
                if part == "q":
                    fn, tt = finish_heads(rope[kind], full, HEADS, q, gq, (g, "q"), parity), qtiles
                elif part == "k":
                    fn, tt = finish_heads(rope[kind], full, HEADS, k, gk, (g, "k"), parity), tiles
                elif part == "v":
                    fn, tt = finish_v(full, CH, v, (g, "v"), parity), tiles
                else:
                    heads = finish_heads(rope[kind], slice(0, 2 * HD), 2, k, gk, (g, "k"), parity)
                    fn, tt = finish_v(slice(2 * HD, CH), 2 * HD, v, (g, "v"), parity, then=heads), tiles
                project(w[l, c0 + n], tt, fn)
            side_work.append(attention(l, g, kind, kvh, q, k, v, qtiles, parity))
        for g in range(4):
            if g == 3:
                side_all()
            project(w[l, 10 + g], qtiles, finish_gate(g))
        side_all()
        mixed_end = T.last()
        group_free[0] = group_free[1] = (mixed_end,)
        done = []
        nt = len(qtiles)
        for f in range(KT):
            tb = banks[3 + f % 4]
            for t in qtiles:
                p1 = T.do(lambda e, f=f, t=t, tb=tb: e.transpose(tb[:, t * P:(t + 1) * P], hid[:, t, f * P:(f + 1) * P], ident),
                          head_ready[(f // 4, "mix", t)], tb.free, mark=t == qtiles[-1])
            tb.free = copy_out(feat[:, f, 0:nt * P], tb[:, 0:nt * P], p1, mixed_end)
            done.append(tb.free)
        state["feat_ready"] = done
        hid_free = p1
        if l < DEPTH - 1:
            have_old = load_ctx.start(S, ctx_old, A["ctx"], mixed_end)
        y_ready = {}

        def finish_y(c):
            def finish(t, bank, done):
                cut = slice(c * CH, (c + 1) * CH)
                p1 = S.do(lambda e: e.activation(scratch, bank[:, :], ACT.Square, accum_out=ssq[:, 4 * t + c:4 * t + c + 1]),
                          done, state["scratch"])
                state["scratch"] = p1
                bank.free = V.do(lambda e: e.tensor_copy(hid[:, t, cut], bank[:, :]), p1, hid_free)
                y_ready[t] = (bank.free, p1)
            return finish
        for c in range(4):
            project(A["w_out"][l, c], qtiles, finish_y(c))
        state["feat"] = T.last()
        state["hid_free"] = T.last()
        new_h = {}
        for t in qtiles:
            p1 = V.do(lambda e, t=t: e.tensor_reduce(rstd[:, t:t + 1], ssq[:, 4 * t:4 * t + 4], AX.X, ALU.add), *y_ready[t])
            p1 = V.do(lambda e, t=t: e.tensor_scalar(rstd[:, t:t + 1], rstd[:, t:t + 1], 1.0 / D, EPS, ALU.mult, ALU.add), p1)
            state[("rstd", t)] = power(rstd[:, t:t + 1], p1)
        for s in range(len(qtiles) // LT):
            for c in range(4):
                cut = slice(c * CH, (c + 1) * CH)
                bank = next_acc()
                for j in range(4):
                    p1 = T.do(lambda e, bank=bank, j=j, c=c, s=s: e.matmul(
                        bank[:, j * P:(j + 1) * P], mod_cols[:, 2 * KT + 4 * c + j, s:s + 1].broadcast_to((P, P)), ident,
                        start=True, stop=True), bank.free, state["gate_ready"], mark=j == 3)
                for t in (LT * s, LT * s + 1):
                    old = h_lat[:, t, cut] if s == 0 else ctx_old[:, t - LT, cut]
                    new = h_lat[:, t, cut] if s == 0 else hid[:, t, cut]
                    y = hid[:, t, cut]
                    p2 = V.do(lambda e, y=y, t=t, bank=bank: e.scalar_tensor_tensor(
                        out=y, in0=y, scalar=rstd[:, t:t + 1], in1=bank[:, :], op0=ALU.mult, op1=ALU.mult),
                        p1, state[("rstd", t)], *y_ready[t])
                    bank.free = p2
                    new_h[t] = G.do(lambda e, new=new, old=old, y=y: e.tensor_tensor(new, old, y, ALU.add),
                                    p2, have_old if s else None)
        state["mod_t"] = p1
        state["h"] = [new_h.get(t) for t in range(NT)]
        state["consts_free"] = ((V.sem, V.count), mixed_end)

    layer_consts(0)
    modulation(0)
    state["h"] = [have_x, have_x, have_ctx, have_ctx]
    for l in range(DEPTH):
        pre_norm(l)
        layer(l)
        if l < DEPTH - 1:
            S.wait(state["mod"])
            V.wait(state["mod_s"], state["mod_t"])
            layer_consts(l + 1)
            modulation(l + 1)

    h_done = state["h"][0:LT]
    ends = [(q.sem, q.count) for q in (V, S, G, T)]
    first_top = top[0]
    h_words = (h_lat[:, 0, 0:1])
    lat_at = common_top + NCONST1 + NT * D + KT * NT * P
    top[0] = common_top
    block_consts[0] = room(NCONST2)
    h_t = room3(KT, T2)
    x_t = room3(KT, T2)
    spare = lat_at - top[0]
    print("spare", spare)
    q_nope = room3(MH, TQ)
    q_pe = room3(MH // 2, TQ)
    k_nope = room3(MH, T2)
    qa_t = room3(QL // P, T2)
    kva_t = room3(KL // P, T2)
    assert top[0] <= lat_at
    top[0] = lat_at + LT * D
    u_t = room3(ST, T2)
    k_pe = room(T2)
    v_rows = room3(3, MH * HD)
    bt_re, bt_im = room3(ST, P), room3(ST, P)
    c_re, c_im = room3(SJ, 32), room3(SJ, 32)
    y_t = room3(ST, T2)
    o_t = x_t[:, ST:2 * ST, :]
    sq = [room(T2) for _ in range(2)]
    rb = room(T2)
    mp = [room(T2) for _ in range(2)]
    mpt = room3(3, P)
    pe_tmp = room(T2)
    print("second block words", top[0])
    scan = {}
    for name in ("trig", "p1", "p2", "q1", "q2"):
        scan[name] = room3(2, T2)
    scan["v"] = room3(2, T2)
    scan["g"] = room3(2, T2)
    scan["h"] = room3(2, T2)
    par = {n: room(SJ) for n in ("dt", "ar", "ph", "e1", "r", "sn", "cs", "hs", "nr", "ni", "den", "cr", "ci", "t1", "t2")}
    print("second block words", top[0])
    meta_rows = scan["p1"].tensor if False else None

    for q in (V, S, G, T):
        q.wait(*ends, *h_done)

    S.wait(load_c.start(S, block_consts[0], A["consts_2"]))
    for q in (V, G, T):
        q.wait((load_c.sem, load_c.count))
    load_b = Load(sem("ssm_loaded"))
    meta = v_rows.rearrange("p a b -> p (a b)")[0:META, 0:D]
    load_meta = Load(sem("meta_loaded"))
    have_meta = load_meta.start(S, meta, A["meta"])
    bc_in = [sq, None]
    b_in = v_rows.rearrange("p a b -> p (a b)")
    raw = scan["p1"].rearrange("p a b -> p (a b)")[:, 0:CH]
    raw_bre, raw_bim = raw, scan["p2"].rearrange("p a b -> p (a b)")[:, 0:CH]
    raw_cre, raw_cim = scan["q1"].rearrange("p a b -> p (a b)")[:, 0:CH], scan["q2"].rearrange("p a b -> p (a b)")[:, 0:CH]
    for dst, name in ((raw_bre, "b_re"), (raw_bim, "b_im"), (raw_cre, "c_re"), (raw_cim, "c_im")):
        have_b = load_b.start(S, dst, A[name])

    h_ready = []
    for f in range(KT):
        tb = banks[3 + f % 5]
        T.do(lambda e, f=f, tb=tb: e.transpose(tb[:, 0:META], meta[:, f * P:(f + 1) * P], ident[0:META, 0:META]),
             have_meta, tb.free, mark=False)
        for t in range(LT):
            p1 = T.do(lambda e, f=f, t=t, tb=tb: e.transpose(tb[:, META + t * P:META + (t + 1) * P],
                                                             h_lat[:, t, f * P:(f + 1) * P], ident), mark=t == 1)
        tb.free = copy_out(h_t[:, f, :], tb[:, 0:T2], p1)
        h_ready.append(tb.free)
    meta_free = p1

    sq_free = [None, None]
    sq_turn = [0]

    def norm_rows(src, n, width, ready, gain, dst, t0, t1, free=None, dst_t0=None):
        bank = next_acc()
        w = t1 - t0
        for f in range(n):
            b = sq_turn[0] % 2
            sq_turn[0] += 1
            p1 = S.do(lambda e, f=f, b=b: e.activation(sq[b][:, 0:w], src[:, f, t0:t1], ACT.Square), ready[f], sq_free[b])
            sq_free[b] = T.do(lambda e, f=f, b=b: e.matmul(bank[:, 0:w], ones, sq[b][:, 0:w], start=f == 0, stop=f == n - 1),
                              p1, bank.free)
        r = rb[:, 0:w]
        p1 = V.do(lambda e: e.tensor_scalar(r, bank[:, 0:w], 1.0 / width, EPS, ALU.mult, ALU.add), sq_free[b], scan.get("rb_free"))
        bank.free = p1
        p1 = power(r, p1)
        done = []
        d0 = t0 if dst_t0 is None else dst_t0
        for f in range(n):
            done.append(V.do(lambda e, f=f: e.scalar_tensor_tensor(
                out=dst[:, f, d0:d0 + w], in0=src[:, f, t0:t1], scalar=col(gain, f), in1=r, op0=ALU.mult, op1=ALU.mult),
                p1, ready[f], free))
        scan["rb_free"] = done[-1]
        return done

    lre, lim, ldt = vec("lam_re"), vec("lam_im"), vec("log_dt")
    k = par

    def v2(fn, *pts):
        return V.do(fn, *pts)
    p1 = S.do(lambda e: e.activation(k["dt"], ldt, ACT.Exp))
    p2 = V.do(lambda e: e.tensor_tensor(k["ar"], lre, k["dt"], ALU.mult), p1)
    p3 = V.do(lambda e: e.tensor_tensor(k["ph"], lim, k["dt"], ALU.mult))
    p4 = S.do(lambda e: e.activation(k["t1"], k["ar"], ACT.Tanh, scale=0.5), p2)
    p5 = S.do(lambda e: e.activation(k["t2"], k["t1"], ACT.Abs), p4)
    p6 = S.do(lambda e: e.activation(k["e1"], k["ar"], ACT.Exp))
    p7 = V.do(lambda e: e.tensor_scalar(k["e1"], k["e1"], 1.0, 2.0, ALU.max, ALU.mult), p6)
    p8 = V.do(lambda e: e.tensor_scalar(k["t2"], k["t2"], 1.0, None, ALU.add), p5)
    p8 = V.do(lambda e: e.reciprocal(k["t2"], k["t2"]), p8)
    p8 = V.do(lambda e: e.tensor_tensor(k["t2"], k["t2"], k["t1"], ALU.mult), p8)
    p8 = V.do(lambda e: e.tensor_tensor(k["e1"], k["e1"], k["t2"], ALU.mult), p8)
    p8 = V.do(lambda e: e.tensor_scalar(k["r"], k["e1"], 1.0, None, ALU.add), p8)
    p9 = V.do(lambda e: e.tensor_scalar(k["ph"], k["ph"], 1.0 / (2.0 * math.pi), None, ALU.mult), p3)
    p9 = V.do(lambda e: e.tensor_scalar(k["t1"], k["ph"], HALF_UP, -HALF_UP, ALU.add, ALU.add), p9, p8)
    p9 = V.do(lambda e: e.tensor_tensor(k["ph"], k["ph"], k["t1"], ALU.subtract), p9)
    p10 = S.do(lambda e: e.activation(k["sn"], k["ph"], ACT.Sin, scale=TWO_PI), p9)
    p11 = S.do(lambda e: e.activation(k["hs"], k["ph"], ACT.Sin, scale=TWO_PI / 2))
    p11 = S.do(lambda e: e.activation(k["hs"], k["hs"], ACT.Square), p11)
    p12 = V.do(lambda e: e.tensor_scalar(k["hs"], k["hs"], 2.0, None, ALU.mult), p11)
    p13 = V.do(lambda e: e.tensor_scalar(k["cs"], k["hs"], -1.0, 1.0, ALU.mult, ALU.add), p12)
    p13 = V.do(lambda e: e.tensor_tensor(k["nr"], k["e1"], k["cs"], ALU.mult), p13)
    p13 = V.do(lambda e: e.tensor_tensor(k["nr"], k["nr"], k["hs"], ALU.subtract), p13)
    p14 = V.do(lambda e: e.tensor_tensor(k["ni"], k["r"], k["sn"], ALU.mult), p10)
    pd = V.do(lambda e: e.tensor_tensor(k["den"], lre, lre, ALU.mult))
    pe_ = V.do(lambda e: e.tensor_tensor(k["t1"], lim, lim, ALU.mult), p14)
    pd = V.do(lambda e: e.tensor_tensor(k["den"], k["den"], k["t1"], ALU.add), pe_)
    pd = V.do(lambda e: e.reciprocal(k["den"], k["den"]), pd)
    for name, (a, b, op) in {"cr": ("nr", "ni", ALU.add), "ci": ("ni", "nr", ALU.subtract)}.items():
        pd = V.do(lambda e, name=name, a=a: e.tensor_tensor(k[name], k[a], lre, ALU.mult), pd)
        pd = V.do(lambda e, b=b: e.tensor_tensor(k["t1"], k[b], lim, ALU.mult), pd)
        pd = V.do(lambda e, name=name, op=op: e.tensor_tensor(k[name], k[name], k["t1"], op), pd)
        pd = V.do(lambda e, name=name: e.tensor_tensor(k[name], k[name], k["den"], ALU.mult), pd)
    coef_ready = pd

    bd = scan["v"].rearrange("p a b -> p (a b)")

    def j3(ap):
        return ap.rearrange("p (j c) -> p j c", c=16)
    blocks = y_t.rearrange("p a b -> p (a b)")[:, 0:2 * SJ * 32].rearrange("p (m j s c) -> p m j s c", m=2, j=SJ, s=2)
    z1 = G.do(lambda e: e.memset(y_t.rearrange("p a b -> p (a b)"), 0.0))
    tm = scan["g"].rearrange("p a b -> p (a b)")[:, 0:CH]
    tm2 = scan["h"].rearrange("p a b -> p (a b)")[:, 0:CH]
    crb, cib = bc(k["cr"], 2, (P, SJ, 16)), bc(k["ci"], 2, (P, SJ, 16))
    pd = None
    for m, (x1, x2, op) in enumerate(((raw_bre, raw_bim, ALU.subtract), (raw_bim, raw_bre, ALU.add))):
        pa = V.do(lambda e, x1=x1: e.tensor_tensor(j3(tm), j3(x1), crb, ALU.mult), coef_ready, have_b, pd)
        pb_ = V.do(lambda e, x2=x2: e.tensor_tensor(j3(tm2), j3(x2), cib, ALU.mult))
        for s in range(2):
            half = slice(s * SUB, (s + 1) * SUB)
            pd = V.do(lambda e, m=m, s=s, half=half, op=op: e.tensor_tensor(
                blocks[half, m, :, s, :], j3(tm[half]), j3(tm2[half]), op), pa, pb_, z1)
    for m, dst in enumerate((bt_re, bt_im)):
        for i in range(ST):
            if i % 4 == 0:
                tb = banks[3 + (2 * m + i // 4) % 4]
            src = blocks[:, m, 4 * i:4 * i + 4, :, :].rearrange("p j s c -> p (j s c)")
            p1 = T.do(lambda e, i=i, tb=tb, src=src: e.transpose(tb[:, (i % 4) * P:(i % 4 + 1) * P], src, ident),
                      pd, tb.free, mark=i % 4 == 3)
            if i % 4 == 3:
                tb.free = copy_out(dst[:, i - 3:i + 1, :], tb[:, :].rearrange("p (i q) -> p i q", q=P), p1)
                scan[("bt", m, i // 4)] = tb.free
    blocks_free = p1
    z2 = G.do(lambda e: e.memset(c_re, 0.0))
    z2 = G.do(lambda e: e.memset(c_im, 0.0))
    for s in range(2):
        half = slice(s * SUB, (s + 1) * SUB)
        p1 = V.do(lambda e, s=s, half=half: e.tensor_copy(c_re[half, :, s * 16:s * 16 + 16], j3(raw_cre[half])), z2, have_b)
        c_ready = V.do(lambda e, s=s, half=half: e.tensor_scalar(c_im[half, :, s * 16:s * 16 + 16], j3(raw_cim[half]),
                                                                 -1.0, None, ALU.mult))
    raw_free = c_ready

    xn = norm_rows(h_t, KT, D, h_ready, "mix_g", x_t, 0, T2)

    def columns(w, kt, m, x, ready, t0, t1, bank, here, first=True, mark_all=False):
        for k_ in range(kt):
            done = T.do(lambda e, k_=k_: e.matmul(bank[0:m, 0:t1 - t0], w[:, k_ * m:(k_ + 1) * m], x[:, k_, t0:t1],
                                                  start=k_ == 0, stop=k_ == kt - 1),
                        here, bank.free, ready[k_], mark=k_ == kt - 1)
            if k_ % 8 == 7:
                side()
        return done

    u_ready, qa_ready, kva_ready = [], [], []
    scan_state = {"buf": None}

    def scan_steps():
        steps = const("steps")
        f = {n: scan[n] for n in ("trig", "p1", "p2", "v", "g", "q1", "q2", "h")}
        free = {n: raw_free for n in f}
        free["v"] = free["g"] = free["h"] = pd
        free_h = None
        bur_b, bui_b, yb = banks[3], banks[4], banks[7]

        def trig(j):
            t = f["trig"]
            x, w = f["q1"], f["q2"]
            pts = (free["trig"], free["q1"], free["q2"])
            a1 = V.do(lambda e: e.tensor_scalar(x[:, 1, :], steps, k["ph"][:, j:j + 1], None, ALU.mult), *pts)
            a2 = V.do(lambda e: e.tensor_scalar(x[:, 0, :], steps, k["ph"][:, j:j + 1], 0.25, ALU.mult, ALU.add))
            a3 = V.do(lambda e: e.tensor_scalar(w, x, HALF_UP, -HALF_UP, ALU.add, ALU.add), a2, a1)
            a4 = V.do(lambda e: e.tensor_tensor(x, x, w, ALU.subtract), a3)
            a5 = S.do(lambda e: e.activation(t, x, ACT.Sin, scale=TWO_PI), a4, free["trig"])
            return a5
        for j in range(SJ):
            i, q4 = j // 4, j % 4
            rows = slice(32 * q4, 32 * q4 + 32)
            tr = trig(j)
            cs = f["trig"]
            b1 = T.do(lambda e, i=i, rows=rows: e.matmul(bur_b[:, 0:T2], bt_re[rows, i, :], u_t[rows, i, :], start=True, stop=True),
                      u_ready[i], bur_b.free, scan[("bt", 0, 0)], scan[("bt", 0, 1)])
            b2 = T.do(lambda e, i=i, rows=rows: e.matmul(bui_b[:, 0:T2], bt_im[rows, i, :], u_t[rows, i, :], start=True, stop=True),
                      u_ready[i], bui_b.free, scan[("bt", 1, 0)], scan[("bt", 1, 1)])
            yield
            c1 = V.do(lambda e: e.tensor_tensor(f["p1"], bc(bur_b[:, 0:T2], 1, (P, 2, T2)), cs, ALU.mult), b1, tr, free["p1"])
            c2 = V.do(lambda e: e.tensor_tensor(f["p2"], bc(bui_b[:, 0:T2], 1, (P, 2, T2)), cs, ALU.mult), b2, tr, free["p2"])
            bur_b.free, bui_b.free = c1, c2
            d1 = G.do(lambda e: e.tensor_tensor(f["v"][:, 0, :], f["p1"][:, 0, :], f["p2"][:, 1, :], ALU.add), c2, free["v"])
            d2 = G.do(lambda e: e.tensor_tensor(f["v"][:, 1, :], f["p2"][:, 0, :], f["p1"][:, 1, :], ALU.subtract), c2)
            free["p1"] = free["p2"] = d2
            rr = k["r"][:, j:j + 1].broadcast_to((P, T2))
            s1 = V.do(lambda e, rr=rr: e.tensor_tensor_scan(f["g"][:, 0, :], rr, f["v"][:, 0, :], 0.0, ALU.mult, ALU.add), d1, free["g"])
            s2 = V.do(lambda e, rr=rr: e.tensor_tensor_scan(f["g"][:, 1, :], rr, f["v"][:, 1, :], 0.0, ALU.mult, ALU.add), d2)
            free["v"] = s2
            e1 = V.do(lambda e: e.tensor_tensor(f["q1"], bc(f["g"][:, 0, :], 1, (P, 2, T2)), cs, ALU.mult), s1)
            e2 = V.do(lambda e: e.tensor_tensor(f["q2"], bc(f["g"][:, 1, :], 1, (P, 2, T2)), cs, ALU.mult), s2)
            free["g"] = e2
            free["trig"] = e2
            g1 = G.do(lambda e: e.tensor_tensor(f["h"][:, 0, :], f["q1"][:, 0, :], f["q2"][:, 1, :], ALU.subtract), e2, free["h"])
            g2 = G.do(lambda e: e.tensor_tensor(f["h"][:, 1, :], f["q1"][:, 1, :], f["q2"][:, 0, :], ALU.add))
            free["q1"] = free["q2"] = g2
            yield
            y1 = T.do(lambda e, j=j, rows=rows: e.matmul(yb[rows, 0:T2], c_re[:, j, :], f["h"][:, 0, :], start=True, stop=False,
                                                         tile_position=(0, rows.start)),
                      g2, c_ready, yb.free, mark=False)
            y2 = T.do(lambda e, j=j, rows=rows: e.matmul(yb[rows, 0:T2], c_im[:, j, :], f["h"][:, 1, :], start=False, stop=True,
                                                         tile_position=(0, rows.start)))
            free["h"] = y2
            if q4 == 3:
                yy, tt_ = y_t[:, i, :], f["p1"][:, 0, :]
                w = V.do(lambda e, i=i, yy=yy: e.scalar_tensor_tensor(out=yy, in0=u_t[:, i, :], scalar=col("d_skip", i),
                                                                      in1=yb[:, 0:T2], op0=ALU.mult, op1=ALU.add), y2, blocks_free)
                yb.free = w
                w2 = S.do(lambda e, yy=yy: e.activation(tt_, yy, ACT.Square), w, free["p1"])
                w2 = V.do(lambda e: e.tensor_scalar(tt_, tt_, 0.044715, 1.0, ALU.mult, ALU.add), w2)
                w2 = V.do(lambda e, yy=yy: e.tensor_tensor(tt_, tt_, yy, ALU.mult), w2)
                w2 = S.do(lambda e: e.activation(tt_, tt_, ACT.Tanh, scale=math.sqrt(2.0 / math.pi)), w2)
                w2 = V.do(lambda e: e.tensor_scalar(tt_, tt_, 1.0, 0.5, ALU.add, ALU.mult), w2)
                w2 = V.do(lambda e, yy=yy: e.tensor_tensor(yy, yy, tt_, ALU.mult), w2)
                free["p1"] = w2
                g_ready.append(w2)
            yield

    g_ready = []
    for ct in range(15):
        m = P if ct < 14 else 64
        w, here, i = piece(A["w_in2"][ct] if ct < 14 else A["w_kpe"], KT * m)
        bank = next_acc()
        done = columns(w, KT, m, x_t, xn, 0, T2, bank, here)
        slot_free[i] = done
        if ct < 8:
            bank.free = S.do(lambda e, ct=ct, bank=bank: e.activation(u_t[:, ct, :], bank[:, 0:T2], ACT.Copy), done)
            u_ready.append(bank.free)
            if ct == 7:
                side_work.append(scan_steps())
        elif ct < 12:
            bank.free = S.do(lambda e, ct=ct, bank=bank: e.activation(qa_t[:, ct - 8, :], bank[:, 0:T2], ACT.Copy), done)
            qa_ready.append(bank.free)
        elif ct < 14:
            bank.free = S.do(lambda e, ct=ct, bank=bank: e.activation(kva_t[:, ct - 12, :], bank[:, 0:T2], ACT.Copy), done)
            kva_ready.append(bank.free)
        else:
            kp = pe_tmp[0:64, :]
            bank.free = kpe_in = S.do(lambda e, bank=bank: e.activation(kp, bank[0:64, 0:T2], ACT.Copy), done)
    x_used = done

    def turn_pe(src, rows, m1, m2, dst, t0, ready):
        w = T2 - t0
        ba, bb = next_acc(), next_acc()
        a1 = T.do(lambda e: e.matmul(ba[:, 0:w], m1, src, start=True, stop=True), ready, ba.free)
        a2 = T.do(lambda e: e.matmul(bb[:, 0:w], m2, src, start=True, stop=True), ready, bb.free)
        t = sq[sq_turn[0] % 2][:, 0:w]
        b_ = sq_turn[0] % 2
        sq_turn[0] += 1
        c1 = V.do(lambda e: e.tensor_tensor(dst, ba[:, 0:w], const("pe_cos")[:, t0:T2], ALU.mult), a1)
        ba.free = c1
        c2 = V.do(lambda e: e.tensor_tensor(t, bb[:, 0:w], const("pe_sin")[:, t0:T2], ALU.mult), a2, sq_free[b_])
        bb.free = c2
        c3 = V.do(lambda e: e.tensor_tensor(dst, dst, t, ALU.add), c2, c1)
        sq_free[b_] = c3
        return c3, a2

    pr = slice(0, 64)
    kpe_ready, _ = turn_pe(kp, 64, const("pe_pair")[pr, :], const("pe_turn_pair")[pr, :], k_pe, 0, kpe_in)
    kp_free = _
    qa_n = norm_rows(qa_t, QL // P, QL, qa_ready, "qa_g", qa_t, 0, T2)
    kva_n = norm_rows(kva_t, KL // P, KL, kva_ready, "kva_g", kva_t, 0, T2)
    qn_ready, qp_ready = [], []
    for grp in range(3):
        w, here, i = piece(A["w_q"][grp])
        for s in range(4):
            bank = next_acc()
            done = columns(w[:, s * CH:(s + 1) * CH], 4, P, qa_t, qa_n, Q0, T2, bank, here)
            side(2)
            if grp < 2:
                h = grp * 4 + s
                bank.free = S.do(lambda e, h=h, bank=bank: e.activation(q_nope[:, h, :], bank[:, 0:TQ], ACT.Copy), done)
                qn_ready.append(bank.free)
            else:
                src = pe_tmp[:, 0:TQ]
                bank.free = S.do(lambda e, bank=bank, src=src: e.activation(src, bank[:, 0:TQ], ACT.Copy), done, kp_free)
                r, kp_free = turn_pe(src, P, ident, const("pe_turn"), q_pe[:, s, :], Q0, bank.free)
                qp_ready.append(r)
        slot_free[i] = done
    w, here, i = piece(A["w_kn"])
    kn_ready = []
    for h in range(MH):
        bank = next_acc()
        done = columns(w[:, h * 2 * P:(h + 1) * 2 * P], 2, P, kva_t, kva_n, 0, T2, bank, here)
        side(1)
        bank.free = S.do(lambda e, h=h, bank=bank: e.activation(k_nope[:, h, :], bank[:, 0:T2], ACT.Copy), done)
        kn_ready.append(bank.free)
    slot_free[i] = done
    w, here, i = piece(A["w_v"])
    v_ready = []
    key_tiles = [(0, P), (P, 2 * P), (2 * P, T2)]
    for c in range(2):
        for n, (a, b) in enumerate(key_tiles):
            bank = next_acc()
            for k_ in range(2):
                done = T.do(lambda e, k_=k_, a=a, b=b, c=c, bank=bank, w=w: e.matmul(
                    bank[0:b - a, :], kva_t[:, k_, a:b], w[:, k_ * 1024 + c * CH:k_ * 1024 + (c + 1) * CH],
                    start=k_ == 0, stop=k_ == 1), here, bank.free, kva_n[k_], mark=k_ == 1)
            bank.free = S.do(lambda e, n=n, c=c, a=a, b=b, bank=bank: e.activation(
                v_rows[0:b - a, n, c * CH:(c + 1) * CH], bank[0:b - a, :], ACT.Copy), done, meta_free)
            v_ready.append(bank.free)
            side(1)
    slot_free[i] = done
    v_all = v_ready[-1]

    mscale = 1.0 / math.sqrt(128 + 64)
    mcols = [cols(4) for _ in range(4)]
    mp_free = [None, None]
    mpt_free = [None]
    un = [0]
    o_ready = []
    mexp = [None] * 4
    tiles2 = [(2, P, META + P), (2 + P, P, T2), (0, 2, META)]
    for h in range(MH):
        ob = next_acc()
        hp = slice((h % 2) * 64, (h % 2) * 64 + 64)
        for n, (a, rows_, keys) in enumerate(tiles2):
            u = un[0] % 2
            m = mcols[un[0] % 4]
            old = mexp[un[0] % 4]
            sb = banks[5]
            T.do(lambda e, h=h, a=a, rows_=rows_, keys=keys: e.matmul(sb[0:rows_, 0:keys], q_nope[:, h, a:a + rows_],
                                                                     k_nope[:, h, 0:keys], start=True, stop=False),
                 qn_ready[h], kn_ready[h], sb.free, mark=False)
            p1 = T.do(lambda e, h=h, a=a, rows_=rows_, keys=keys, hp=hp: e.matmul(
                sb[0:rows_, 0:keys], q_pe[hp, h // 2, a:a + rows_], k_pe[hp, 0:keys], start=False, stop=True),
                qp_ready[h // 2], kpe_ready)
            pr_ = mp[u][0:rows_, 0:keys]
            if rows_ == P:
                mask = const("mla_mask")[:, n * T2:n * T2 + keys]
                p2 = V.do(lambda e, pr_=pr_, keys=keys, mask=mask: e.scalar_tensor_tensor(
                    out=pr_, in0=sb[:, 0:keys], scalar=mscale, in1=mask, op0=ALU.mult, op1=ALU.add), p1, mp_free[u])
            else:
                p2 = V.do(lambda e, pr_=pr_, keys=keys, rows_=rows_: e.tensor_scalar(
                    pr_, sb[0:rows_, 0:keys], mscale, None, ALU.mult), p1, mp_free[u])
            sb.free = p2
            mm = m[0:rows_]
            p3 = V.do(lambda e, mm=mm, pr_=pr_: e.tensor_reduce(mm[:, 0:1], pr_, AX.X, ALU.max), p2, old)
            p3 = V.do(lambda e, mm=mm: e.tensor_scalar(mm[:, 0:1], mm[:, 0:1], -1.0, None, ALU.mult), p3)
            p4 = S.do(lambda e, mm=mm, pr_=pr_: e.activation(pr_, pr_, ACT.Exp, bias=mm[:, 0:1], accum_out=mm[:, 1:2]), p3)
            mexp[un[0] % 4] = p4
            p5 = V.do(lambda e, mm=mm: e.reciprocal(mm[:, 2:3], mm[:, 1:2]), p4)
            p5 = V.do(lambda e, mm=mm, pr_=pr_: e.tensor_scalar(pr_, pr_, mm[:, 2:3], None, ALU.mult), p5)
            side(1)
            tb = banks[6]
            kts = [(x, min(x + P, keys)) for x in range(0, keys, P)]
            for j, (x0, x1) in enumerate(kts):
                p6 = T.do(lambda e, j=j, x0=x0, x1=x1, pr_=pr_, rows_=rows_: e.transpose(
                    tb[0:x1 - x0, j * P:j * P + rows_], pr_[:, x0:x1], ident[0:rows_, 0:rows_]), p5, tb.free, mark=j == len(kts) - 1)
            mp_free[u] = p6
            for j, (x0, x1) in enumerate(kts):
                tb.free = p7 = S.do(lambda e, j=j, x0=x0, x1=x1, rows_=rows_: e.activation(
                    mpt[0:x1 - x0, j, 0:rows_], tb[0:x1 - x0, j * P:j * P + rows_], ACT.Copy), p6, mpt_free[0])
            side(1)
            for j, (x0, x1) in enumerate(kts):
                p8 = T.do(lambda e, j=j, x0=x0, x1=x1, a=a, rows_=rows_, h=h, ob=ob, kts=kts: e.matmul(
                    ob[:, a:a + rows_], v_rows[0:x1 - x0, j, h * HD:(h + 1) * HD], mpt[0:x1 - x0, j, 0:rows_],
                    start=j == 0, stop=j == len(kts) - 1), p7, ob.free, v_all, mark=j == len(kts) - 1)
            mpt_free[0] = p8
            un[0] += 1
        ob.free = S.do(lambda e, h=h, ob=ob: e.activation(o_t[:, h, 0:TQ], ob[:, 0:TQ], ACT.Copy), p8, x_used)
        o_ready.append(ob.free)
    side_all()

    ys = x_t[:, 0:ST, :]
    ya_ready = []
    half_b = cols(ST)
    hb = V.do(lambda e: e.tensor_scalar(half_b, vec("b_glu"), 0.5, None, ALU.mult))
    for pr2 in range(4):
        w, here, i = piece(A["w_glu"][pr2])
        for s in range(2):
            ct = 2 * pr2 + s
            bank = next_acc()
            done = columns(w[:, s * 1024:(s + 1) * 1024], ST, P, y_t, g_ready, Q0, T2, bank, here)
            d = ys[:, ct, 0:TQ]
            w1 = S.do(lambda e, d=d, ct=ct, bank=bank: e.activation(d, bank[:, 0:TQ], ACT.Tanh, scale=0.5, bias=half_b[:, ct:ct + 1]),
                      done, hb, x_used)
            bank.free = w1
            w1 = V.do(lambda e, d=d: e.tensor_scalar(d, d, 1.0, 0.5, ALU.add, ALU.mult), w1)
            w1 = V.do(lambda e, d=d, ct=ct: e.tensor_tensor(d, d, y_t[:, ct, Q0:T2], ALU.mult), w1)
            ya_ready.append(w1)
        slot_free[i] = done
    na_ = norm_rows(ys, ST, DS, ya_ready, "ssm_g", ys, 0, TQ)
    nb_ = norm_rows(o_t, ST, DS, o_ready, "attn_g", o_t, 0, TQ)
    cat = na_ + nb_
    h2 = []
    for ct in range(KT):
        w, here, i = piece(A["w_out2"][ct])
        bank = next_acc()
        done = columns(w, KT, P, x_t, cat, 0, TQ, bank, here)
        slot_free[i] = done
        bank.free = V.do(lambda e, ct=ct, bank=bank: e.tensor_tensor(h_t[:, ct, Q0:T2], h_t[:, ct, Q0:T2], bank[:, 0:TQ], ALU.add),
                         done, h_ready[ct])
        h2.append(bank.free)
    xf = norm_rows(h_t, KT, D, h2, "ffn_g", x_t, Q0, T2, free=done)
    ends = [(q.sem, q.count) for q in (V, S, G, T)]
    top[0] = common_top + NCONST2 + 2 * KT * T2
    act_t = room3(FT, LAT)
    g_sb = [[room(LAT) for _ in range(2)] for _ in range(2)]
    h_rows = room3(LT, D)
    fin_g = room(D)
    sc2 = room(CH)
    print("third part words", top[0])
    for q in (V, S, G):
        q.wait(*ends)
    load_fin = Load(sem("final_loaded"))
    have_fin = load_fin.start(S, fin_g, A["final_g"])
    hr = {}
    for t in range(LT):
        for c in range(4):
            tb = banks[3 + (4 * t + c) % 4]
            for j in range(4):
                p1 = T.do(lambda e, t=t, c=c, j=j, tb=tb: e.transpose(
                    tb[:, j * P:(j + 1) * P], h_t[:, 4 * c + j, META + t * P:META + (t + 1) * P], ident),
                    h2[4 * c + j], tb.free, mark=j == 3)
            tb.free = copy_out(h_rows[:, t, c * CH:(c + 1) * CH], tb[:, :], p1)
            hr[(t, c)] = tb.free
    a_ready = []
    gfree = [None, None]
    for f in range(FT):
        wg, hg, ig = piece(A["w_up"][f])
        wv, hv, iv = piece(A["w_up"][FT + f])
        bg, bv = banks[(2 * f) % 4], banks[(2 * f + 1) % 4]
        dg = columns(wg, KT, P, x_t, xf, Q0, T2, bg, hg)
        slot_free[ig] = dg
        dv = columns(wv, KT, P, x_t, xf, META, T2, bv, hv)
        slot_free[iv] = dv
        u = f % 2
        a, b = g_sb[u]
        w0, w1, w2 = (col("conv_w", kk * FT + f) for kk in range(CONVW))
        p1 = S.do(lambda e, a=a, bg=bg, w2=w2, f=f: e.activation(a, bg[:, 2:2 + LAT], ACT.Identity, scale=w2, bias=col("conv_b", f)),
                  dg, gfree[u])
        p1 = V.do(lambda e, a=a, bg=bg, w1=w1: e.scalar_tensor_tensor(out=a, in0=bg[:, 1:1 + LAT], scalar=w1, in1=a,
                                                                     op0=ALU.mult, op1=ALU.add), p1)
        p1 = V.do(lambda e, a=a, bg=bg, w0=w0: e.scalar_tensor_tensor(out=a, in0=bg[:, 0:LAT], scalar=w0, in1=a,
                                                                     op0=ALU.mult, op1=ALU.add), p1)
        bg.free = p1
        p2 = S.do(lambda e, a=a, b=b: e.activation(b, a, ACT.Tanh, scale=0.5), p1, gfree[u])
        p2 = V.do(lambda e, a=a, b=b: e.scalar_tensor_tensor(out=b, in0=b, scalar=1.0, in1=a, op0=ALU.add, op1=ALU.mult), p2)
        p2 = V.do(lambda e, b=b, bv=bv, f=f: e.scalar_tensor_tensor(out=act_t[:, f, :], in0=bv[:, 0:LAT], scalar=0.5, in1=b,
                                                                    op0=ALU.mult, op1=ALU.mult), p2, dv)
        bv.free = p2
        gfree[u] = p2
        a_ready.append(p2)
    store = Load(sem("stored"))
    ssf = cols(LT * 4)
    rsf = cols(LT)
    yd = {}
    for c in range(4):
        bk = [banks[4 + 2 * (c % 2)], banks[5 + 2 * (c % 2)]]
        for kg in range(11):
            n = 4 if kg < 10 else 3
            w, here, i = piece(A["w_down"][c, kg] if n == 4 else A["w_down_end"][c], n * CH)
            for k_ in range(n):
                kk = 4 * kg + k_
                for t in range(LT):
                    done = T.do(lambda e, w=w, k_=k_, kk=kk, t=t, bk=bk: e.matmul(
                        bk[t][:, :], act_t[:, kk, t * P:(t + 1) * P], w[:, k_ * CH:(k_ + 1) * CH],
                        start=kk == 0, stop=kk == FT - 1), here, bk[t].free, a_ready[kk], mark=t == 1 and k_ == n - 1)
            slot_free[i] = done
        cut = slice(c * CH, (c + 1) * CH)
        for t in range(LT):
            p1 = V.do(lambda e, t=t, bk=bk, cut=cut: e.tensor_tensor(h_rows[:, t, cut], h_rows[:, t, cut], bk[t][:, :], ALU.add),
                      done, hr[(t, c)])
            bk[t].free = p1
            yd[(t, c)] = p1
            yd[("s", t)] = S.do(lambda e, t=t, cut=cut, c=c: e.activation(sc2, h_rows[:, t, cut], ACT.Square,
                                                                         accum_out=ssf[:, 4 * t + c:4 * t + c + 1]), p1, yd.get("sc"))
            yd["sc"] = yd[("s", t)]
    last = None
    for t in range(LT):
        r = rsf[:, t:t + 1]
        p1 = V.do(lambda e, t=t, r=r: e.tensor_reduce(r, ssf[:, 4 * t:4 * t + 4], AX.X, ALU.add), yd[("s", t)])
        p1 = V.do(lambda e, r=r: e.tensor_scalar(r, r, 1.0 / D, EPS, ALU.mult, ALU.add), p1)
        p1 = power(r, p1)
        for c in range(4):
            cut = slice(c * CH, (c + 1) * CH)
            p2 = V.do(lambda e, t=t, r=r, cut=cut: e.scalar_tensor_tensor(
                out=h_rows[:, t, cut], in0=h_rows[:, t, cut], scalar=r, in1=fin_g[:, cut], op0=ALU.mult, op1=ALU.mult),
                p1, have_fin, yd[("s", t)])
            last = store.start(Y, out[0, t * P:(t + 1) * P, cut], h_rows[:, t, cut], p2)
    Y.wait(last)

    with nc.Block() as block:
        @block.sync
        def _(e):
            Y.emit(e)

        @block.scalar
        def _(e):
            S.emit(e)

        @block.gpsimd
        def _(e):
            G.emit(e)

        @block.vector
        def _(e):
            V.emit(e)

        @block.tensor
        def _(e):
            T.emit(e)


def shape_constants():
    parts = [np.zeros((P, n), np.float32) for n in (NCONST, NCONST1, NCONST2)]

    def put(name, a):
        lo, hi = CONST[name]
        c = parts[0 if name in BOTH else 1 if name in FIRST_ONLY else 2]
        a = np.asarray(a, np.float32)
        c[:a.shape[0], lo:hi] = a.reshape(a.shape[0], hi - lo)
    put("ident", np.eye(P))
    put("ones", np.ones((P, P)))
    tok = np.arange(LAT)
    for name, dim in (("s", SUB), ("h", HD)):
        nf = dim // 4
        inv = (np.float32(10000.0) ** (-np.arange(nf, dtype=np.float32) / np.float32(nf))).astype(np.float32)
        row, col_ = (tok // GRID).astype(np.float32), (tok % GRID).astype(np.float32)
        ang = np.concatenate([row[:, None] * inv, col_[:, None] * inv], -1).astype(np.float32)
        for fn, what in ((np.cos, "cos_"), (np.sin, "sin_")):
            put(what + name, fn(ang).reshape(LT, P, -1).transpose(1, 0, 2))
    q, k = tok[:, None], tok[None, :]
    win = np.where(np.abs(k - q) <= 128, 0.0, MASKED)
    put("win_mask", win.reshape(LT, P, LAT).transpose(1, 0, 2))
    start = np.clip(q % GRID - 8, 0, GRID - 16)
    na = np.where((k % GRID >= start) & (k % GRID < start + 16), 0.0, MASKED)
    put("na_mask", na.reshape(LT, P, LAT).transpose(1, 0, 2))
    pos = np.arange(T2)
    chunk = np.where(pos < META, 0, 1 + (pos - META) // 64)
    mm = np.where(chunk[None, :] <= chunk[META:, None], 0.0, MASKED)
    put("mla_mask", mm.reshape(LT, P, T2).transpose(1, 0, 2))
    turn = np.zeros((64, 64), np.float32)
    for i in range(32):
        turn[32 + i, i] = -1.0
        turn[i, 32 + i] = 1.0
    both = np.zeros((P, P), np.float32)
    both[:64, :64] = turn
    both[64:, 64:] = turn
    put("pe_turn", both)
    put("pe_pair", np.tile(np.eye(64), (1, 2)))
    put("pe_turn_pair", np.tile(turn, (1, 2)))
    inv = (1.0 / (np.float32(10000.0) ** (np.arange(0, 64, 2, dtype=np.float32) / np.float32(64)))).astype(np.float32)
    ang = (pos.astype(np.float32)[:, None] * inv[None, :]).astype(np.float32).T
    put("pe_cos", np.tile(np.cos(ang), (4, 1)))
    put("pe_sin", np.tile(np.sin(ang), (4, 1)))
    put("steps", np.broadcast_to(pos, (P, T2)))
    put("minus_half", np.full((P, 1), -0.5))
    return parts


def lay_out(i):
    f = {n: np.asarray(a) for n, a in i.items()}

    def tiles(a):
        return a.reshape(-1, P).T
    parts = {
        "pre_g": tiles(f["pre_norm_g"].reshape(-1)), "post_g": tiles(f["post_norm_g"].reshape(-1)), "b_mod": tiles(f["b_mod"].reshape(-1)),
        "sink": np.broadcast_to(f["win_sink"].reshape(1, -1), (P, 2 * HEADS)),
        "silu_in": np.stack([tiles(f["c"][0]), tiles(f["c_ctx"])], -1).reshape(P, -1),
        "lambda_in": np.broadcast_to(np.stack([f["diff_lambda_q1"], f["diff_lambda_k1"], f["diff_lambda_q2"],
                                               f["diff_lambda_k2"]], 1).reshape(1, -1), (P, 2 * 4 * SUB)),
        "mix_g": tiles(f["mix_norm_2"][0]), "ffn_g": tiles(f["ffn_norm_2"][0]), "b_glu": tiles(f["b_glu_2"][0]),
        "d_skip": tiles(f["d_skip_2"][0]), "qa_g": tiles(f["q_a_norm_2"][0]), "kva_g": tiles(f["kv_a_norm_2"][0]),
        "ssm_g": tiles(f["out_norm_ssm_2"][0]), "attn_g": tiles(f["out_norm_attn_2"][0]),
        "conv_w": tiles(f["conv_w_2"][0].reshape(-1)), "conv_b": tiles(f["conv_b_2"][0]),
        "lam_re": tiles(f["lam_re_2"][0].reshape(-1)), "lam_im": tiles(f["lam_im_2"][0].reshape(-1)),
        "log_dt": tiles(np.repeat(f["log_dt_2"][0], SUB)),
    }
    vectors = np.concatenate([parts[n] for n in VEC], 1)

    def moving(w, n):
        return w.reshape(-1, 4, P, n, CH).transpose(3, 0, 2, 1, 4).reshape(n, -1, P, PIECE)

    def still(w):
        k = w.shape[0] // P
        return w.reshape(k, P, -1, P).transpose(2, 1, 0, 3).reshape(w.shape[1] // P, P, k * P)
    tok = np.arange(LAT)
    q, k = tok[:, None], tok[None, :]
    rpb = f["na_rpb"]
    bias = rpb[:, :, (k // GRID) - (q // GRID) + 7, np.clip(k % GRID - q % GRID + 15, 0, 30)]
    w_q = f["w_q_b_2"][0].reshape(QL, MH, 192)
    w_q = np.concatenate([w_q[:, :, :P].reshape(QL, -1), w_q[:, :, P:].reshape(QL, -1)], 1)
    w_kv = f["w_kv_b_2"][0].reshape(KL, MH, 256)
    w2 = f["w_in_2"][0]
    down = f["w_down_2"][0]
    consts, consts_1, consts_2 = shape_constants()
    a = {
        "vectors": vectors, "consts": consts, "consts_1": consts_1, "consts_2": consts_2,
        "x": f["x"][0].reshape(LT, P, D).transpose(1, 0, 2), "ctx": f["ctx"][0].reshape(LT, P, D).transpose(1, 0, 2),
        "meta": f["meta_tokens_2"],
        "w_mod": np.stack([moving(w, MODC) for w in f["w_mod"]]),
        "w_in": np.stack([moving(w, INC) for w in f["w_in"]]),
        "w_out": np.stack([moving(w, 4) for w in f["w_out"]]),
        "gate_bias": np.broadcast_to(f["b_mod"][:, None, 2 * D:], (DEPTH, 2, D)),
        "post_g": np.broadcast_to(f["post_norm_g"][:, None], (DEPTH, 2, D)),
        "subln": np.broadcast_to(f["diff_subln_g"][:, None], (DEPTH, P, HD)),
        "qk_g": np.broadcast_to(np.stack([f["qk_q_norm_g"], f["qk_k_norm_g"]], 1)[:, None], (DEPTH, P, 2, HD)),
        "na_bias": bias.reshape(DEPTH, HEADS, LT, P, LAT).transpose(0, 3, 1, 2, 4).reshape(DEPTH, P, HEADS * LT, LAT),
        "w_in2": still(w2[:, :14 * P]),
        "w_kpe": w2[:, 14 * P:].reshape(KT, P, 64).transpose(1, 0, 2).reshape(P, KT * 64),
        "w_q": still(w_q).reshape(3, 4, P, CH).transpose(0, 2, 1, 3).reshape(3, P, PIECE),
        "w_kn": still(w_kv[:, :, :P].reshape(KL, -1)).transpose(1, 0, 2).reshape(P, PIECE),
        "w_v": w_kv[:, :, P:].reshape(2, P, 1024).transpose(1, 0, 2).reshape(P, PIECE),
        "w_glu": still(f["w_glu_2"][0]).reshape(4, 2, P, 1024).transpose(0, 2, 1, 3).reshape(4, P, PIECE),
        "w_out2": still(f["w_out_2"][0]), "w_up": still(f["w_up_2"][0]),
        "w_down": moving(down[:40 * P], 4),
        "w_down_end": down[40 * P:].reshape(3, P, 4, CH).transpose(2, 1, 0, 3).reshape(4, P, 3 * CH),
        "b_re": f["b_re_2"][0].reshape(SJ, P, 16).transpose(1, 0, 2).reshape(P, CH),
        "b_im": f["b_im_2"][0].reshape(SJ, P, 16).transpose(1, 0, 2).reshape(P, CH),
        "c_re": f["c_re_2"][0].reshape(SJ, 2, 16, SUB).transpose(1, 3, 0, 2).reshape(P, CH),
        "c_im": f["c_im_2"][0].reshape(SJ, 2, 16, SUB).transpose(1, 3, 0, 2).reshape(P, CH),
        "final_g": np.broadcast_to(f["final_norm_2"][None], (P, D)),
    }
    return {n: np.ascontiguousarray(x) for n, x in a.items()}


def kernel(**inputs):
    import concourse.bacc as bacc
    from concourse.bass_utils import run_bass_kernel_spmd as run

    nc = bacc.Bacc("TRN2", target_bir_lowering=False, num_devices=1)
    arrays = lay_out(inputs)
    aps = {n: nc.dram_tensor(n, a.shape, mybir.dt.from_np(a.dtype), kind="ExternalInput").ap() for n, a in arrays.items()}
    out = nc.dram_tensor("out", (1, LAT, D), F32, kind="ExternalOutput").ap()
    build(nc, aps, out)
    r = run(nc, [arrays], core_ids=[0])
    return r.results[0]["out"]
```

```python
import math

import numpy as np

import concourse.bass as bass
from concourse import mybir

F32 = mybir.dt.float32
F32R = mybir.dt.float32r
ALU = mybir.AluOpType
ACT = mybir.ActivationFunctionType
AX = mybir.AxisListType

P = 128
D = 2048
KT = D // P
DEPTH = 2
LAT, CTX = 256, 256
NT = (LAT + CTX) // P
LT = LAT // P
GRID = 64
HD = 128
HEADS = 4
SUB = 64
CH = 512
MODC = 3 * D // CH
INC = 14
EPS = 1e-6
MASKED = -1e30
PIECE = 1024
RAW = 3
HALVES = 3
KP = PIECE // CH
MODRING = 3

META = 16
T2 = META + LAT
Q0 = META - 2
TQ = T2 - Q0
DS = 1024
ST = DS // P
SJ = 32
MH = 8
QL, KL = 512, 256
FF = 5504
FT = FF // P
CONVW = 3
HALF_UP = 12582912.0
TWO_PI = 6.283185

VEC = {}


def _columns():
    at = 0
    for name, n in (("pre_g", 2 * KT), ("post_g", 2 * KT), ("b_mod", 2 * 3 * KT), ("sink", 2 * HEADS),
                    ("silu_in", 2 * KT),
                    ("mix_g", KT), ("ffn_g", KT), ("b_glu", ST), ("d_skip", ST), ("qa_g", QL // P), ("kva_g", KL // P),
                    ("ssm_g", ST), ("attn_g", ST), ("conv_w", CONVW * FT), ("conv_b", FT),
                    ("lam_re", SJ), ("lam_im", SJ), ("log_dt", SJ)):
        VEC[name] = (at, at + n)
        at += n
    return at


NVEC = _columns()

CONST = {}


def _constants(*entries):
    at = 0
    for name, n in entries:
        CONST[name] = (at, at + n)
        at += n
    return at


NCONST = _constants(("ident", P), ("ones", P), ("minus_half", 1))
NCONST1 = _constants(("cos_h", LT * SUB), ("sin_h", LT * SUB), ("cos_s", LT * 32), ("sin_s", LT * 32),
                     ("win_mask", LT * LAT))
NCONST2 = _constants(("mla_mask", LT * T2), ("pe_turn", P), ("pe_cos", T2), ("pe_sin", T2))
FIRST_ONLY = ("cos_h", "sin_h", "cos_s", "sin_s", "win_mask")
BOTH = ("ident", "ones", "minus_half")



class Queue:

    def __init__(self, sem):
        self.sem, self.count, self.todo, self.seen = sem, 0, [], {}

    def wait(self, *points):
        for point in points:
            if point is None:
                continue
            sem, count = point
            if self.seen.get(sem.name, 0) < count:
                self.seen[sem.name] = count
                self.todo.append(lambda e, s=sem, c=count: e.wait_ge(s, c))

    def do(self, make, *points, mark=True):
        self.wait(*points)
        if not mark:
            self.todo.append(make)
            return None
        self.count += 1
        self.todo.append(lambda e, s=self.sem: make(e).then_inc(s, 1))
        return (self.sem, self.count)

    def last(self):
        return (self.sem, self.count)

    def emit(self, engine):
        for make in self.todo:
            make(engine)


class Load:

    def __init__(self, sem):
        self.sem, self.count = sem, 0

    def start(self, queue, dst, src, *points):
        queue.wait(*points)
        self.count += 16
        queue.todo.append(lambda e, s=self.sem: e.dma_start(dst, src).then_inc(s, 16))
        return (self.sem, self.count)

    def last(self):
        return (self.sem, self.count)


class Bank:

    def __init__(self, tensor):
        self.t, self.free = tensor, None

    def __getitem__(self, key):
        return self.t[key]


def bc(ap, axis, shape):
    return ap.unsqueeze(axis).broadcast_to(shape)


def weight_plan(A):
    plan = [("raw", PIECE, A["w_mod"][c, g]) for c in range(2 * MODC // 3) for g in range(KT // KP)]

    def add(pieces):
        plan.extend(("split", piece.shape[-1], piece) for piece in pieces)

    for l in range(DEPTH):
        for c in (0, 1, 2, 10, 3, 4, 11, 5, 6, 7, 12, 8, 9, 13):
            add(A["w_in"][l, c, g] for g in range(KT // KP))
        for c in range(4):
            add(A["w_out"][l, c, g] for g in range(KT // KP))
    for c in range(14):
        add(A["w_in2"][c, g] for g in range(2))
    add(A["w_kpe"][0, g] for g in range(2))
    add(A["w_q"][g] for g in range(MH * 192 // P // 2))
    add(A["w_kn"][g] for g in range(2))
    add(A["w_v"][c, 0] for c in range(2))
    add(A["w_glu"][c] for c in range(ST))
    for c in range(KT):
        add(A["w_out2"][c, g] for g in range(2))
    for f in range(FT):
        add(A["w_up"][half * FT + f, g] for half in range(2) for g in range(2))
    for c in range(4):
        add(A["w_down"][c, g] for g in range(FT // KP))
        add([A["w_down_end"][c]])
    return plan


def build(nc, A, out):

    def sem(name):
        return nc.semaphore(name).__enter__()

    V, S, G, T, Y = (Queue(sem(n)) for n in ("vector_done", "scalar_done", "gpsimd_done", "tensor_done", "sync_done"))

    def tensor(name, words, dtype=F32):
        held = nc.sbuf_tensor(name, [P, words], dtype)
        return held, held.__enter__()

    class Room:

        def __init__(self, t, words, at=0):
            self.t, self.words, self.at = t, words, at

        def one(self, words):
            at = self.at
            self.at += words
            assert self.at <= self.words, (self.at, self.words)
            return self.t[:, at:at + words]

        def two(self, a, b):
            return self.one(a * b).rearrange("p (a b) -> p a b", b=b)

    banks = [Bank(nc.psum_tensor(f"bank{i}", [P, CH], F32).__enter__()) for i in range(8)]

    small_words = 200
    common_words = RAW * PIECE + NCONST + NVEC + 2 * 3 * KT * 2 + 2 * KT * 2 + small_words + 4 * SJ
    _, common_t = tensor("common", common_words + KT * T2)
    _, split_t = tensor("split_weights", 2 * HALVES * PIECE, F32R)
    C = Room(common_t, common_words)
    raw_slots = C.two(RAW, PIECE)
    consts = C.one(NCONST)
    block_consts = [None]
    vecs = C.one(NVEC)
    split_slots = split_t[:, :].rearrange("p (s i w) -> p s i w", s=2, i=HALVES)
    h_t_words = common_t[:, common_words:common_words + KT * T2]

    def const(name):
        return (consts if name in BOTH else block_consts[0])[:, CONST[name][0]:CONST[name][1]]

    def vec(name):
        return vecs[:, VEC[name][0]:VEC[name][1]]

    def col(name, i):
        return vecs[:, VEC[name][0] + i:VEC[name][0] + i + 1]

    ident, ones = const("ident"), const("ones")
    mod_all = [C.two(3 * KT, 2) for _ in range(DEPTH)]
    scaled_g_all = [C.two(KT, 2) for _ in range(DEPTH)]
    ssm_r, ssm_ph, ssm_cr, ssm_ci = (C.one(SJ) for _ in range(4))
    small = C.one(small_words)
    small_at = [0]

    def cols(n):
        at = small_at[0]
        small_at[0] += n
        assert small_at[0] <= small_words
        return small[:, at:at + n]

    plan = weight_plan(A)
    raw_loads = [Load(sem(f"raw{i}_loaded")) for i in range(RAW)]
    raw_have, raw_free, split_have = {}, {}, {}
    split_free = [None] * HALVES
    stream = {"load": 0, "split": 0, "take": 0}

    def start_loads():
        while stream["load"] < len(plan):
            m = stream["load"]
            if m >= RAW and m - RAW not in raw_free:
                return
            _, words, src = plan[m]
            raw_have[m] = raw_loads[m % RAW].start(Y, raw_slots[:, m % RAW, 0:words], src, raw_free.get(m - RAW))
            stream["load"] += 1

    split_count = [0]

    def split_next():
        m = stream["split"]
        kind, words, _ = plan[m]
        if kind == "raw":
            stream["split"] += 1
            return
        i = split_count[0] % HALVES
        split_count[0] += 1
        raw = raw_slots[:, m % RAW, 0:words]
        hi, lo = split_slots[:, 0, i, 0:words], split_slots[:, 1, i, 0:words]
        p_hi = S.do(lambda e: e.activation(hi, raw, ACT.Copy), raw_have[m], split_free[i])
        p_lo = V.do(lambda e: e.tensor_tensor(lo, raw, hi.bitcast(F32), ALU.subtract), p_hi, raw_have[m], split_free[i])
        raw_free[m] = p_lo
        split_have[m] = (hi, lo, p_lo, i)
        stream["split"] += 1

    def take(kind):
        n = stream["take"]
        assert plan[n][0] == kind, (n, plan[n][0], kind)
        stream["take"] += 1
        start_loads()
        while stream["split"] < len(plan) and stream["split"] <= n + HALVES - 1:
            if stream["split"] not in raw_have:
                break
            split_next()
            start_loads()
        if kind == "split":
            return split_have.pop(n)
        return raw_slots[:, n % RAW, 0:plan[n][1]], raw_have[n], n

    turned = []
    side_work = []
    background = []
    clock = [0]
    every = 2

    def advance(works):
        try:
            next(works[0])
        except StopIteration:
            works.pop(0)

    def advance_if(works):
        if works:
            advance(works)

    def side(n=1):
        for _ in range(n):
            clock[0] += 1
            if turned:
                if turned[0][0] < clock[0]:
                    turned.pop(0)[1]()
            elif side_work:
                advance(side_work)
            if background and clock[0] % every == 0:
                advance(background)

    def side_all():
        while turned or side_work:
            side()

    flip = [0]

    def copy_out(dst, src, *points):
        flip[0] ^= 1
        if flip[0]:
            return S.do(lambda e: e.activation(dst, src, ACT.Copy), *points)
        return V.do(lambda e: e.tensor_copy(dst, src), *points)

    load_c, load_v, load_x = Load(sem("consts_loaded")), Load(sem("vectors_loaded")), Load(sem("x_loaded"))
    load_ctx, load_bias = Load(sem("ctx_loaded")), Load(sem("bias_loaded"))
    have_v = load_v.start(S, vecs, A["vectors"])
    have_c = load_c.start(S, consts, A["consts"])
    for q in (V, G, T, S):
        q.wait(have_v, have_c)

    old_held, old_t = tensor("old_stream", NT * D)
    old_h = old_t[:, :].rearrange("p (a b) -> p a b", b=D)
    R = Room(old_t, NT * D)
    q_t, k_t, v_all_rows = R.two(HEADS, NT * P), R.two(HEADS, NT * P), R.two(NT, CH)
    na_bias = R.two(HEADS * LT, LAT)
    feat_held, feat_r = tensor("features", 2 * KT * NT * P, F32R)
    feat = feat_r[:, :].rearrange("p (s k t) -> p s k t", s=2, k=KT)
    work_words = NT * D + NCONST1 + 3 * CH + KT * 2 + MODRING * CH + 2 * CH + 3 * HD
    work_held, work_t = tensor("first_block_work", work_words)
    W = Room(work_t, work_words)
    hid = W.two(NT, D)
    block_consts[0] = W.one(NCONST1)
    rows_buf = [W.one(CH) for _ in range(2)]
    scratch = W.one(CH)
    silu_c = W.two(KT, 2)
    mod_ring = W.two(MODRING, CH)
    mod_acc = [W.one(CH) for _ in range(2)]
    subln = W.one(HD)
    qk_g = W.two(2, HD)
    H = Room(h_t_words, KT * T2)
    probs_a = [H.one(CH) for _ in range(2)]
    probs_b = H.one(CH)
    probs_t = [H.one(CH) for _ in range(2)]
    mod_tmp = H.one(CH)
    turn_a, turn_b = H.one(CH), H.one(CH)

    ssq, rstd = cols(NT * 4), cols(NT)
    lam_col, lam_t = cols(1), cols(4)
    mx = [cols(4) for _ in range(4)]
    sums = [cols(HEADS) for _ in range(2)]
    rinv = [cols(HEADS) for _ in range(2)]
    dif = [cols(4) for _ in range(2)]
    hss = cols(HEADS * 2)

    have_c = load_c.start(S, block_consts[0], A["consts_1"])
    have_x = load_x.start(S, old_h[:, 0:LT, :], A["x"])
    have_ctx = load_ctx.start(S, old_h[:, LT:NT, :], A["ctx"])
    for q in (V, G, S):
        q.wait(have_c)

    c_in = vec("silu_in").rearrange("p (k s) -> p k s", s=2)
    p = S.do(lambda e: e.activation(silu_c, c_in, ACT.Tanh, scale=0.5))
    p = V.do(lambda e: e.scalar_tensor_tensor(out=silu_c, in0=silu_c, scalar=1.0, in1=c_in, op0=ALU.add, op1=ALU.mult), p)
    silu_ready = V.do(lambda e: e.tensor_scalar(silu_c, silu_c, 0.5, None, ALU.mult), p)

    state = {"feat_free": None, "hid_free": None, "scratch": None, "h": [have_x, have_x, have_ctx, have_ctx]}
    flip_acc, acc_banks = [3], [4]

    def next_acc():
        flip_acc[0] = (flip_acc[0] + 1) % acc_banks[0]
        return banks[flip_acc[0]]

    def mod_column(l, c, points, sums_in):
        b0 = VEC["b_mod"][0] + l * 3 * KT + 4 * c
        return V.do(lambda e: e.tensor_tensor(mod_all[l][:, 4 * c:4 * c + 4, :], sums_in,
                                              bc(vecs[:, b0:b0 + 4], 2, (P, 4, 2)), ALU.add), *points)

    def mod_end(l, part, point):
        if part == "scale":
            sg = scaled_g_all[l]
            g0 = VEC["pre_g"][0] + l * KT
            p1 = V.do(lambda e: e.tensor_scalar(sg, mod_all[l][:, KT:2 * KT, :], 1.0, None, ALU.add), point)
            state[("mod", l)] = V.do(lambda e: e.tensor_tensor(sg, sg, bc(vecs[:, g0:g0 + KT], 2, (P, KT, 2)), ALU.mult), p1)
        else:
            gate = mod_all[l][:, 2 * KT:, :]
            state[("gate", l)] = V.do(lambda e: e.tensor_tensor(
                gate, gate, bc(vec("post_g")[:, l * KT:(l + 1) * KT], 2, (P, KT, 2)), ALU.mult), point)

    def modulation_first():
        for c in range(2 * MODC // 3):
            bank = next_acc()
            for kg in range(KT // KP):
                w, here, n = take("raw")
                for k in range(KP):
                    kk = KP * kg + k
                    done = T.do(lambda e, w=w, k=k, kk=kk, bank=bank: e.matmul(
                        bank[0:2, :], silu_c[:, kk, :], w[:, k * CH:(k + 1) * CH], start=kk == 0, stop=kk == KT - 1),
                        here, silu_ready, bank.free, mark=k == KP - 1)
                raw_free[n] = done
                start_loads()
            r = scratch[0:2, :]
            bank.free = V.do(lambda e, b=bank: e.tensor_copy(r, b[0:2, :]), done, state["scratch"])
            tb = banks[4 + c % 2]
            for j in range(4):
                t = T.do(lambda e, j=j, tb=tb: e.transpose(tb[:, 2 * j:2 * j + 2], r[:, j * P:(j + 1) * P], ident[0:2, 0:2]),
                         bank.free, tb.free, mark=j == 3)
            state["scratch"] = t
            tb.free = mod_column(0, c, (t,), tb[:, 0:8].rearrange("p (j s) -> p j s", s=2))
            for _ in range(SJ // (2 * MODC // 3) + 1):
                advance_if(tables)
        mod_end(0, "scale", tb.free)

    mod_loads = [Load(sem(f"mod{i}_loaded")) for i in range(MODRING)]
    mod_have, mod_free = {}, {}
    acc_free = [None]

    def modulation_rest():
        todo = [(0, c, k) for c in range(2 * MODC // 3, MODC) for k in range(KT)]
        todo += [(l, c, k) for l in range(1, DEPTH) for c in range(MODC) for k in range(KT)]

        def load(m):
            if m < len(todo):
                l, c, k = todo[m]
                mod_have[m] = mod_loads[m % MODRING].start(S, mod_ring[:, m % MODRING, :], A["w_mod_rows"][l, c, k],
                                                           *mod_free.get(m - MODRING, ()))
        for m in range(MODRING - 1):
            load(m)
        p_lat = p_ctx = None
        for m, (l, c, k) in enumerate(todo):
            w = mod_ring[:, m % MODRING, :]
            x_lat, x_ctx = silu_c[:, k, 0:1], silu_c[:, k, 1:2].broadcast_to((P, CH))
            with_ctx = l < DEPTH - 1 or c < 2 * MODC // 3
            if k == 0:
                p_lat = V.do(lambda e, w=w, x=x_lat: e.tensor_scalar(mod_acc[0], w, x, None, ALU.mult),
                             mod_have[m], acc_free[0], silu_ready)
            else:
                p_lat = V.do(lambda e, w=w, x=x_lat: e.scalar_tensor_tensor(
                    out=mod_acc[0], in0=w, scalar=x, in1=mod_acc[0], op0=ALU.mult, op1=ALU.add), mod_have[m], p_lat)
            if with_ctx:
                o = mod_acc[1] if k == 0 else mod_tmp
                p_w = p_ctx = G.do(lambda e, w=w, x=x_ctx, o=o: e.tensor_tensor(o, w, x, ALU.mult),
                                   mod_have[m], acc_free[0], silu_ready, p_ctx)
                if k > 0:
                    p_ctx = G.do(lambda e: e.tensor_tensor(mod_acc[1], mod_acc[1], mod_tmp, ALU.add), p_w)
            mod_free[m] = (p_lat, p_w) if with_ctx else (p_lat,)
            load(m + MODRING - 1)
            yield
            if k == KT - 1:
                tb = banks[6]
                for j in range(4):
                    for s in range(2):
                        x = mod_acc[s if with_ctx else 0][:, j * P:(j + 1) * P]
                        t = T.do(lambda e, j=j, s=s, x=x: e.matmul(tb[:, 2 * j + s:2 * j + s + 1], x, ones[:, 0:1],
                                                                   start=True, stop=True),
                                 p_lat, p_ctx, tb.free, mark=j == 3 and s == 1)
                acc_free[0] = t
                tb.free = mod_column(l, c, (t,), tb[:, 0:8].rearrange("p (j s) -> p j s", s=2))
                if c == 2 * MODC // 3 - 1:
                    mod_end(l, "scale", tb.free)
                if c == MODC - 1:
                    mod_end(l, "gate", tb.free)
                yield

    load_gains, load_lam, load_mask = Load(sem("gains_loaded")), Load(sem("lambda_loaded")), Load(sem("mask_loaded"))

    def layer_consts(l):
        before = (*state.get("consts_free", ()), *state["qkv_free"])
        load_gains.start(S, subln, A["subln"][l], *before)
        state["gains"] = load_gains.start(S, qk_g, A["qk_g"][l])
        have = load_bias.start(S, na_bias, A["na_bias"][l])
        mask = scratch
        have_m = load_mask.start(S, mask, A["na_mask"], state["scratch"])
        m = mask.rearrange("p (t k) -> p t k", k=LAT)
        for h in range(HEADS):
            b = na_bias[:, h * LT:(h + 1) * LT, :]
            p1 = V.do(lambda e, b=b: e.tensor_tensor(b, b, m, ALU.add), have, have_m)
        state["na_ready"] = state["scratch"] = p1
        lv = turn_b[:, 0:4 * SUB]
        have = load_lam.start(S, lv, A["lambda_in"][l], state.get("turn_free"), state.get("turn_free2"))
        lv = lv.rearrange("p (v d) -> p v d", d=SUB)
        prod = turn_a[:, 0:2 * SUB].rearrange("p (v d) -> p v d", d=SUB)
        p2 = V.do(lambda e: e.tensor_tensor(prod, lv[:, 0:3:2, :], lv[:, 1:4:2, :], ALU.mult), have)
        p2 = V.do(lambda e: e.tensor_reduce(lam_t[:, 0:2], prod, AX.X, ALU.add), p2)
        p2 = S.do(lambda e: e.activation(lam_t[:, 2:4], lam_t[:, 0:2], ACT.Exp), p2)
        p2 = V.do(lambda e: e.tensor_tensor(lam_col, lam_t[:, 2:3], lam_t[:, 3:4], ALU.subtract), p2)
        lam_init = 0.8 - 0.6 * math.exp(-0.3 * l)
        state["lam"] = V.do(lambda e: e.tensor_scalar(lam_col, lam_col, lam_init, None, ALU.add), p2)
        state["turn_free"] = p2

    def power(dst, *points):
        mh = const("minus_half")[0:dst.shape[0], :].broadcast_to((dst.shape[0], dst.shape[-1]))
        return G.do(lambda e: e.tensor_tensor(dst, dst, mh, ALU.pow), *points)

    def split_into(hi, lo, src, *points):
        a = S.do(lambda e: e.activation(hi, src, ACT.Copy), *points)
        b = V.do(lambda e: e.tensor_tensor(lo, src, hi.bitcast(F32), ALU.subtract), a, *points)
        return a, b

    def pre_norm(l):
        for q in (V, S):
            q.wait(V.last(), G.last())
        scaled = [None] * NT
        sg, mc = scaled_g_all[l], mod_all[l]
        for t in range(NT):
            src, have = old_h[:, t, :], state["h"][t]
            for c in range(4):
                p1 = S.do(lambda e, c=c, src=src, t=t: e.activation(
                    scratch, src[:, c * CH:(c + 1) * CH], ACT.Square, accum_out=ssq[:, 4 * t + c:4 * t + c + 1]),
                    have, state["scratch"])
                state["scratch"] = p1
            p1 = V.do(lambda e, t=t: e.tensor_reduce(rstd[:, t:t + 1], ssq[:, 4 * t:4 * t + 4], AX.X, ALU.add), p1)
            p1 = V.do(lambda e, t=t: e.tensor_scalar(rstd[:, t:t + 1], rstd[:, t:t + 1], 1.0 / D, EPS, ALU.mult, ALU.add), p1)
            p1 = power(rstd[:, t:t + 1], p1)
            scaled[t] = V.do(lambda e, t=t, src=src: e.tensor_scalar(hid[:, t, :], src, rstd[:, t:t + 1], None, ALU.mult),
                             p1, have, state["hid_free"])
        state["old_read"] = scaled[NT - 1]
        done, tmp_free = [], [state.get("turn_free"), state.get("turn_free")]
        for f in range(KT):
            tb = banks[4 + f % 4]
            for t in range(NT):
                p1 = T.do(lambda e, f=f, t=t, tb=tb: e.transpose(tb[:, t * P:(t + 1) * P], hid[:, t, f * P:(f + 1) * P], ident),
                          scaled[t], tb.free, mark=t == NT - 1)
            tmp = (turn_a, turn_b)[f % 2]
            for s in range(2):
                part = slice(s * LAT, (s + 1) * LAT)
                g, b = sg[:, f, s:s + 1], mc[:, f, s:s + 1]
                if f % 2:
                    p2 = S.do(lambda e, tmp=tmp, tb=tb, part=part, g=g, b=b: e.activation(
                        tmp[:, part], tb[:, part], ACT.Identity, scale=g, bias=b), p1, state[("mod", l)], tmp_free[f % 2])
                else:
                    p2 = V.do(lambda e, tmp=tmp, tb=tb, part=part, g=g, b=b: e.tensor_scalar(
                        tmp[:, part], tb[:, part], g, b, ALU.mult, ALU.add), p1, state[("mod", l)], tmp_free[f % 2])
            tb.free = p2
            _, p3 = split_into(feat[:, 0, f, :], feat[:, 1, f, :], tmp, p2, state["feat_free"])
            tmp_free[f % 2] = p3
            done.append(p3)
        state["feat_ready"] = done
        state["turn_free"] = p3
        state["hid_free"] = p1

    def triple(out_ap, xs, ws, first, last, *points, mark=False):
        for n, (a, b) in enumerate(((0, 0), (1, 0), (0, 1))):
            done = T.do(lambda e, a=a, b=b, n=n: e.matmul(out_ap, xs[a], ws[b], start=first and n == 0, stop=last and n == 2),
                        *points, mark=mark and n == 2)
        return done

    def project(tiles, finish):
        accs = {t: next_acc() for t in tiles}
        for kg in range(KT // KP):
            hi, lo, here, i = take("split")
            for t in tiles:
                for k in range(KP):
                    kk = KP * kg + k
                    cols_ = slice(k * CH, (k + 1) * CH)
                    done = triple(accs[t][:, :], (feat[:, 0, kk, t * P:(t + 1) * P], feat[:, 1, kk, t * P:(t + 1) * P]),
                                  (hi[:, cols_], lo[:, cols_]), kk == 0, kk == KT - 1,
                                  here, accs[t].free, state["feat_ready"][kk], mark=k == KP - 1)
                split_free[i] = done
                if kg == KT // KP - 1:
                    finish(t, accs[t], done)
                side()

    row_turn = [0]
    rows_free = [None, None]
    head_ready = {}

    def rotate(x, r, t, nh, sub, points):
        half = (SUB if sub else HD) // 2
        n = nh * 2 if sub else nh
        cs = const("cos_s" if sub else "cos_h")[:, t * half:(t + 1) * half]
        sn = const("sin_s" if sub else "sin_h")[:, t * half:(t + 1) * half]
        w = nh * HD

        def v4(ap):
            return ap.rearrange("p (n s d) -> p n s d", s=2, d=half)
        cosb = cs.unsqueeze(1).unsqueeze(1).broadcast_to((P, n, 2, half))
        sinb = bc(sn, 1, (P, n, half))
        a, b = turn_a[:, 0:w], turn_b[:, 0:w]
        p1 = V.do(lambda e: e.tensor_tensor(v4(a), v4(x), cosb, ALU.mult), *points, state.get("turn_free"), state.get("turn_free2"))
        p2 = V.do(lambda e: e.tensor_tensor(v4(b)[:, :, 0, :], v4(x)[:, :, 1, :], sinb, ALU.mult), *points)
        p3 = V.do(lambda e: e.tensor_tensor(v4(b)[:, :, 1, :], v4(x)[:, :, 0, :], sinb, ALU.mult), *points)
        p4 = G.do(lambda e: e.tensor_tensor(v4(r)[:, :, 0, :], v4(a)[:, :, 0, :], v4(b)[:, :, 0, :], ALU.subtract), p1, p3, *points)
        p5 = G.do(lambda e: e.tensor_tensor(v4(r)[:, :, 1, :], v4(a)[:, :, 1, :], v4(b)[:, :, 1, :], ALU.add), p1, p3)
        state["turn_free"] = p5
        return p3, p5

    def finish_heads(kind, x_cut, nh, dst, gain, key):
        def finish(t, bank, done):
            x = bank[:, x_cut]
            b = row_turn[0] % 2
            row_turn[0] += 1
            w = nh * HD
            r = rows_buf[b][:, 0:w]
            points = (done, rows_free[b])
            if gain is not None:
                def h3(ap):
                    return ap.rearrange("p (h d) -> p h d", d=HD)
                hs = hss[:, 0:nh]
                p1 = S.do(lambda e: e.activation(turn_a[:, 0:w], x, ACT.Square), done, state.get("turn_free"), state.get("turn_free2"))
                p1 = V.do(lambda e: e.tensor_reduce(hs, h3(turn_a[:, 0:w]), AX.X, ALU.add), p1)
                p1 = V.do(lambda e: e.tensor_scalar(hs, hs, 1.0 / HD, EPS, ALU.mult, ALU.add), p1)
                p1 = power(hs, p1)
                p2 = V.do(lambda e: e.tensor_tensor(h3(scratch[:, 0:w]), h3(x), bc(hs, 2, (P, nh, HD)), ALU.mult),
                          p1, done, state["scratch"])
                bank.free = p2
                y = r if t >= LT else scratch[:, 0:w]
                p3 = V.do(lambda e: e.tensor_tensor(h3(y), h3(scratch[:, 0:w]), bc(qk_g[:, gain, :], 1, (P, nh, HD)), ALU.mult),
                          p2, state["gains"], rows_free[b])
                state["scratch"] = p3
                state["turn_free2"] = p2
                if t < LT:
                    read, ready = rotate(y, r, t, nh, False, (p3, rows_free[b]))
                    state["scratch"] = read
                else:
                    ready = p3
            elif t < LT and kind in ("sub", "head"):
                bank.free, ready = rotate(x, r, t, nh, kind == "sub", points)
            else:
                ready = bank.free = S.do(lambda e: e.activation(r, x, ACT.Copy), *points)

            def turn():
                tb = banks[6]
                for h in range(nh):
                    p1 = T.do(lambda e, h=h: e.transpose(tb[:, h * P:(h + 1) * P], r[:, h * P:(h + 1) * P], ident),
                              ready, tb.free, mark=h == nh - 1)
                rows_free[b] = p1
                tb.free = S.do(lambda e: e.activation(dst[:, 0:nh, t * P:(t + 1) * P],
                                                      tb[:, 0:w].rearrange("p (h q) -> p h q", q=P), ACT.Copy),
                               p1, *state["qkv_free"])
                head_ready[(*key, t)] = tb.free
            turned.append((clock[0] + 1, turn))
        return finish

    def finish_v(x_cut, w, v, key, then=None):
        def finish(t, bank, done):
            p1 = V.do(lambda e: e.tensor_copy(v[:, t, 0:w], bank[:, x_cut]), done, *state["qkv_free"])
            head_ready[(*key, t)] = p1
            bank.free = p1
            if then is not None:
                then(t, bank, p1)
        return finish

    unit_no = [0]
    probs_free = [None, None]
    probs_b_free = [None]
    exp_done = [None] * 4
    probs_t_free = [None, None]
    out_turn = [0]
    last_read = {}

    def attention(l, g, kind, kv_heads, q, k, v, tiles):
        scale = (SUB if kind == "diff" else HD) ** -0.5
        lam_init = 0.8 - 0.6 * math.exp(-0.3 * l)
        obank = banks[7]
        units = [(t, h) for t in tiles for h in range(HEADS)]
        work = {}

        def scores(t, h):
            u = unit_no[0] % 2
            m = mx[unit_no[0] % 4]
            older = exp_done[unit_no[0] % 4]
            k0 = 0 if t < LT else LAT
            n = NT * P - k0
            hk = h // (HEADS // kv_heads)
            keys = tuple(head_ready[(g, "k", tt)] for tt in range(k0 // P, NT))
            pa, pb = probs_a[u][:, 0:n], probs_b[:, 0:n]
            sm = sums[t % 2]
            if kind == "diff":
                dd = dif[u]
                es = []
                for s in range(2):
                    sb = banks[4 + s]
                    p1 = T.do(lambda e, s=s, sb=sb: e.matmul(
                        sb[:, 0:n], q[s * SUB:(s + 1) * SUB, h, t * P:(t + 1) * P], k[s * SUB:(s + 1) * SUB, hk, k0:NT * P],
                        start=True, stop=True), head_ready[(g, "q", t)], *keys, sb.free)
                    p2 = V.do(lambda e, s=s, sb=sb: e.tensor_reduce(m[:, s:s + 1], sb[:, 0:n], AX.X, ALU.max), p1, older)
                    p2 = V.do(lambda e, s=s: e.tensor_scalar(m[:, s:s + 1], m[:, s:s + 1], -scale, None, ALU.mult), p2)
                    o = (pa, pb)[s]
                    sb.free = S.do(lambda e, s=s, sb=sb, o=o: e.activation(
                        o, sb[:, 0:n], ACT.Exp, bias=m[:, s:s + 1], scale=scale, accum_out=dd[:, s:s + 1]),
                        p2, probs_free[u] if s == 0 else probs_b_free[0])
                    es.append(sb.free)
                p3 = V.do(lambda e: e.reciprocal(dd[:, 2:4], dd[:, 0:2]), es[1])
                p4 = V.do(lambda e: e.tensor_scalar(dd[:, 3:4], dd[:, 3:4], lam_col, None, ALU.mult), p3, state["lam"])
                p4 = V.do(lambda e: e.tensor_scalar(pb, pb, dd[:, 3:4], None, ALU.mult), p4)
                p4 = V.do(lambda e: e.scalar_tensor_tensor(out=pa, in0=pa, scalar=dd[:, 2:3], in1=pb,
                                                           op0=ALU.mult, op1=ALU.subtract), p4)
                exp_done[unit_no[0] % 4] = es[1]
                probs_b_free[0] = p4
                work[(t, h)] = (u, pa, p4, k0)
            else:
                sb = banks[4 + u]
                p1 = T.do(lambda e: e.matmul(sb[:, 0:n], q[:, h, t * P:(t + 1) * P], k[:, hk, k0:NT * P],
                                             start=True, stop=True), head_ready[(g, "q", t)], *keys, sb.free)
                src, sc, points = sb[:, 0:n], scale, (p1,)
                biased = t < LT and kind in ("win", "na")
                if biased:
                    bias = (const("win_mask")[:, t * LAT:(t + 1) * LAT] if kind == "win" else na_bias[:, h * LT + t, :])
                    p2 = V.do(lambda e: e.scalar_tensor_tensor(out=pb[:, 0:LAT], in0=sb[:, 0:LAT], scalar=scale, in1=bias,
                                                               op0=ALU.mult, op1=ALU.add),
                              p1, state["na_ready"], probs_b_free[0])
                    sb.free = S.do(lambda e: e.activation(pb[:, LAT:], sb[:, LAT:n], ACT.Copy, scale=scale), p2)
                    src, sc, points = pb, 1.0, (sb.free,)
                p2 = V.do(lambda e: e.tensor_reduce(m[:, 0:1], src, AX.X, ALU.max), *points, older)
                if kind == "win":
                    sink = col("sink", l * HEADS + h)
                    p2 = V.do(lambda e: e.tensor_scalar(m[:, 0:1], m[:, 0:1], sc, sink, ALU.mult, ALU.max), p2)
                    p2 = V.do(lambda e: e.tensor_scalar(m[:, 0:1], m[:, 0:1], -1.0, None, ALU.mult), p2)
                else:
                    p2 = V.do(lambda e: e.tensor_scalar(m[:, 0:1], m[:, 0:1], -sc, None, ALU.mult), p2)
                p3 = S.do(lambda e: e.activation(pa, src, ACT.Exp, bias=m[:, 0:1], scale=sc, accum_out=sm[:, h:h + 1]),
                          p2, probs_free[u], last_read.get(("sums", t % 2)))
                if biased:
                    probs_b_free[0] = p3
                else:
                    sb.free = p3
                summed = p3
                if kind == "win":
                    p4 = S.do(lambda e: e.activation(m[:, 1:2], sink, ACT.Exp, bias=m[:, 0:1]), p2)
                    summed = V.do(lambda e: e.tensor_tensor(sm[:, h:h + 1], sm[:, h:h + 1], m[:, 1:2], ALU.add), p4, p3)
                exp_done[unit_no[0] % 4] = summed if kind != "win" else p4
                last_read[("summed", t % 2)] = summed
                work[(t, h)] = (u, pa, p3, k0)
            unit_no[0] += 1

        def flip_probs(t, h):
            u, pa, ready, k0 = work[(t, h)]
            nk = NT - k0 // P
            tb = banks[6]
            for j in range(nk):
                p1 = T.do(lambda e, j=j: e.transpose(tb[:, j * P:(j + 1) * P], pa[:, j * P:(j + 1) * P], ident),
                          ready, tb.free, mark=j == nk - 1)
            probs_free[u] = p1
            tb.free = copy_out(probs_t[u][:, 0:nk * P], tb[:, 0:nk * P], p1, probs_t_free[u])
            work[(t, h)] = (u, tb.free, k0)

        def values(t, h):
            u, ready, k0 = work[(t, h)]
            nk = NT - k0 // P
            hk = h // (HEADS // kv_heads)
            for j in range(nk):
                kt = k0 // P + j
                p1 = T.do(lambda e, j=j, kt=kt: e.matmul(obank[:, h * HD:(h + 1) * HD], probs_t[u][:, j * P:(j + 1) * P],
                                                         v[:, kt, hk * HD:(hk + 1) * HD], start=j == 0, stop=j == nk - 1),
                          ready, obank.free, head_ready[(g, "v", kt)], mark=j == nk - 1)
            probs_t_free[u] = p1
            if h < HEADS - 1:
                return
            dst = hid[:, t, g * CH:(g + 1) * CH]
            p_gate = gates.get((g, t))
            b = row_turn[0] % 2
            if p_gate is not None:
                row_turn[0] += 1
            o = dst if p_gate is None else rows_buf[b]
            o_free = state["hid_free"] if p_gate is None else rows_free[b]

            def h3(ap):
                return ap.rearrange("p (h d) -> p h d", d=HD)
            if kind == "diff":
                hs = hss[:, HEADS:2 * HEADS]
                p2 = S.do(lambda e: e.activation(o, obank[:, :], ACT.Square), p1, o_free)
                p2 = V.do(lambda e: e.tensor_reduce(hs, h3(o), AX.X, ALU.add), p2)
                p2 = V.do(lambda e: e.tensor_scalar(hs, hs, 1.0 / HD, EPS, ALU.mult, ALU.add), p2)
                p2 = power(hs, p2)
                p2 = V.do(lambda e: e.tensor_tensor(h3(o), h3(obank[:, :]), bc(hs, 2, (P, HEADS, HD)), ALU.mult), p2)
                obank.free = p2
                p2 = V.do(lambda e: e.scalar_tensor_tensor(out=h3(o), in0=h3(o), scalar=1.0 - lam_init,
                                                           in1=bc(subln, 1, (P, HEADS, HD)), op0=ALU.mult, op1=ALU.mult),
                          p2, state["gains"])
            else:
                ri = rinv[t % 2]
                p2 = V.do(lambda e: e.reciprocal(ri, sums[t % 2]), last_read[("summed", t % 2)])
                last_read[("sums", t % 2)] = p2
                p2 = V.do(lambda e: e.tensor_tensor(h3(o), h3(obank[:, :]), bc(ri, 2, (P, HEADS, HD)), ALU.mult),
                          p2, p1, o_free)
                obank.free = p2
            if p_gate is None:
                outputs[(g, t)] = p2
            else:
                head_ready[(g, "mix", t)] = rows_free[b] = V.do(lambda e: e.scalar_tensor_tensor(
                    out=dst, in0=dst, scalar=0.5, in1=o, op0=ALU.mult, op1=ALU.mult), p2, p_gate)

        for i in range(len(units) + 2):
            if i < len(units):
                scores(*units[i])
            if 0 <= i - 1 < len(units):
                flip_probs(*units[i - 1])
            if 0 <= i - 2 < len(units):
                values(*units[i - 2])
            yield
    outputs, gates = {}, {}

    def finish_gate(g):
        def finish(t, bank, done):
            dst = hid[:, t, g * CH:(g + 1) * CH]
            p_o = outputs.get((g, t))
            b = row_turn[0] % 2
            if p_o is not None:
                row_turn[0] += 1
            r = dst if p_o is None else rows_buf[b]
            p1 = S.do(lambda e: e.activation(r, bank[:, :], ACT.Tanh, scale=0.5), done,
                      state["hid_free"] if p_o is None else rows_free[b])
            p2 = V.do(lambda e: e.scalar_tensor_tensor(out=r, in0=r, scalar=1.0, in1=bank[:, :], op0=ALU.add, op1=ALU.mult), p1)
            bank.free = p2
            if p_o is None:
                gates[(g, t)] = p2
            else:
                head_ready[(g, "mix", t)] = rows_free[b] = V.do(lambda e: e.scalar_tensor_tensor(
                    out=dst, in0=r, scalar=0.5, in1=dst, op0=ALU.mult, op1=ALU.mult), p2, p_o)
        return finish

    def layer(l):
        tiles = list(range(NT))
        qtiles = tiles if l < DEPTH - 1 else tiles[:LT]
        plan_ = (("diff", HEADS, ("q", "k", "v")), ("win", 2, ("q", "kv")), ("na", HEADS, ("q", "k", "v")), ("qk", 2, ("q", "kv")))
        rope = {"diff": "sub", "win": "head", "na": None, "qk": "head"}
        full = slice(0, CH)
        state["qkv_free"] = (state["old_read"], state.get("kept"))
        outputs.clear()
        gates.clear()
        for g, (kind, kvh, parts) in enumerate(plan_):
            gq, gk = (0, 1) if kind == "qk" else (None, None)
            for part in parts:
                if part == "q":
                    project(qtiles, finish_heads(rope[kind], full, HEADS, q_t, gq, (g, "q")))
                elif part == "k":
                    project(tiles, finish_heads(rope[kind], full, HEADS, k_t, gk, (g, "k")))
                elif part == "v":
                    project(tiles, finish_v(full, CH, v_all_rows, (g, "v")))
                else:
                    heads = finish_heads(rope[kind], slice(0, 2 * HD), 2, k_t, gk, (g, "k"))
                    project(tiles, finish_v(slice(2 * HD, CH), 2 * HD, v_all_rows, (g, "v"), then=heads))
                if g == 0 and part == "q":
                    layer_consts(l)
            side_work.append(attention(l, g, kind, kvh, q_t, k_t, v_all_rows, qtiles))
            project(qtiles, finish_gate(g))
            side_all()
            state["qkv_free"] = (T.last(),)
        mixed_end = T.last()
        state["consts_free"] = (mixed_end, V.last())
        if l == 0:
            load_x.start(S, old_h[:, 0:LT, :], A["x"], mixed_end, V.last())
            have_old = [(load_x.sem, load_x.count)] * 2 + [load_ctx.start(S, old_h[:, LT:NT, :], A["ctx"])] * 2
        else:
            have_old = [load_x.start(S, old_h[:, 0:LT, :], A["kept_stream"], mixed_end, V.last(), state["kept"])] * 2
        done = []
        nt = len(qtiles)
        for f in range(KT):
            tb = banks[4 + f % 4]
            for t in qtiles:
                p1 = T.do(lambda e, f=f, t=t, tb=tb: e.transpose(tb[:, t * P:(t + 1) * P], hid[:, t, f * P:(f + 1) * P], ident),
                          head_ready[(f // 4, "mix", t)], tb.free, mark=t == qtiles[-1])
            _, tb.free = split_into(feat[:, 0, f, 0:nt * P], feat[:, 1, f, 0:nt * P], tb[:, 0:nt * P], p1, mixed_end)
            done.append(tb.free)
        state["feat_ready"] = done
        hid_free = p1
        y_ready = {}

        def finish_y(c):
            def finish(t, bank, done):
                cut = slice(c * CH, (c + 1) * CH)
                p1 = S.do(lambda e: e.activation(scratch, bank[:, :], ACT.Square, accum_out=ssq[:, 4 * t + c:4 * t + c + 1]),
                          done, state["scratch"])
                state["scratch"] = p1
                bank.free = V.do(lambda e: e.tensor_copy(hid[:, t, cut], bank[:, :]), p1, hid_free)
                y_ready[t] = (bank.free, p1)
            return finish
        for c in range(4):
            project(qtiles, finish_y(c))
        state["feat_free"] = T.last()
        while ("gate", l) not in state or (l < DEPTH - 1 and ("mod", l + 1) not in state):
            advance(background)
        new_h = {}
        for t in qtiles:
            p1 = V.do(lambda e, t=t: e.tensor_reduce(rstd[:, t:t + 1], ssq[:, 4 * t:4 * t + 4], AX.X, ALU.add), *y_ready[t])
            p1 = V.do(lambda e, t=t: e.tensor_scalar(rstd[:, t:t + 1], rstd[:, t:t + 1], 1.0 / D, EPS, ALU.mult, ALU.add), p1)
            state[("rstd", t)] = power(rstd[:, t:t + 1], p1)
        for s in range(len(qtiles) // LT):
            for c in range(4):
                cut = slice(c * CH, (c + 1) * CH)
                bank = next_acc()
                for j in range(4):
                    p1 = T.do(lambda e, bank=bank, j=j, c=c, s=s: e.matmul(
                        bank[:, j * P:(j + 1) * P], mod_all[l][:, 2 * KT + 4 * c + j, s:s + 1].broadcast_to((P, P)), ident,
                        start=True, stop=True), bank.free, state[("gate", l)], mark=j == 3)
                for t in (LT * s, LT * s + 1):
                    h, y = old_h[:, t, cut], hid[:, t, cut]
                    p2 = V.do(lambda e, y=y, t=t, bank=bank: e.scalar_tensor_tensor(
                        out=y, in0=y, scalar=rstd[:, t:t + 1], in1=bank[:, :], op0=ALU.mult, op1=ALU.mult),
                        p1, state[("rstd", t)], *y_ready[t])
                    bank.free = p2
                    new_h[t] = G.do(lambda e, h=h, y=y: e.tensor_tensor(h, h, y, ALU.add), p2, have_old[t])
        state["h"] = [new_h.get(t) for t in range(NT)]
        state["hid_free"] = new_h[qtiles[-1]]
        if l < DEPTH - 1:
            state["kept"] = load_kept.start(S, A["kept_stream"], old_h[:, 0:LT, :], new_h[1])

    store_trig = [Load(sem(f"trig{i}_stored")) for i in range(2)]
    load_steps = Load(sem("steps_loaded"))

    def ssm_tables():
        B = Room(h_t_words, KT * T2)
        k = {n: B.one(SJ) for n in ("dt", "ar", "e1", "sn", "cs", "hs", "nr", "ni", "den", "t1", "t2")}
        k.update(r=ssm_r, ph=ssm_ph, cr=ssm_cr, ci=ssm_ci)
        steps, x, w = B.one(T2), B.two(3, T2), B.two(3, T2)
        out_bufs = [B.two(3, T2) for _ in range(2)]
        have_steps = load_steps.start(S, steps, A["steps"])
        lre, lim, ldt = vec("lam_re"), vec("lam_im"), vec("log_dt")
        p1 = S.do(lambda e: e.activation(k["dt"], ldt, ACT.Exp))
        p2 = V.do(lambda e: e.tensor_tensor(k["ar"], lre, k["dt"], ALU.mult), p1)
        p3 = V.do(lambda e: e.tensor_tensor(k["ph"], lim, k["dt"], ALU.mult))
        p4 = S.do(lambda e: e.activation(k["t1"], k["ar"], ACT.Tanh, scale=0.5), p2)
        p5 = S.do(lambda e: e.activation(k["t2"], k["t1"], ACT.Abs), p4)
        p6 = S.do(lambda e: e.activation(k["e1"], k["ar"], ACT.Exp))
        p7 = V.do(lambda e: e.tensor_scalar(k["e1"], k["e1"], 1.0, 2.0, ALU.max, ALU.mult), p6)
        p8 = V.do(lambda e: e.tensor_scalar(k["t2"], k["t2"], 1.0, None, ALU.add), p5)
        p8 = V.do(lambda e: e.reciprocal(k["t2"], k["t2"]), p8)
        p8 = V.do(lambda e: e.tensor_tensor(k["t2"], k["t2"], k["t1"], ALU.mult), p8)
        p8 = V.do(lambda e: e.tensor_tensor(k["e1"], k["e1"], k["t2"], ALU.mult), p8)
        p8 = V.do(lambda e: e.tensor_scalar(k["r"], k["e1"], 1.0, None, ALU.add), p8)
        p9 = V.do(lambda e: e.tensor_scalar(k["ph"], k["ph"], 1.0 / (2.0 * math.pi), None, ALU.mult), p3)
        p9 = V.do(lambda e: e.tensor_scalar(k["t1"], k["ph"], HALF_UP, -HALF_UP, ALU.add, ALU.add), p9, p8)
        p9 = V.do(lambda e: e.tensor_tensor(k["ph"], k["ph"], k["t1"], ALU.subtract), p9)
        p10 = S.do(lambda e: e.activation(k["sn"], k["ph"], ACT.Sin, scale=TWO_PI), p9)
        p11 = S.do(lambda e: e.activation(k["hs"], k["ph"], ACT.Sin, scale=TWO_PI / 2))
        p11 = S.do(lambda e: e.activation(k["hs"], k["hs"], ACT.Square), p11)
        p12 = V.do(lambda e: e.tensor_scalar(k["hs"], k["hs"], 2.0, None, ALU.mult), p11)
        p13 = V.do(lambda e: e.tensor_scalar(k["cs"], k["hs"], -1.0, 1.0, ALU.mult, ALU.add), p12)
        p13 = V.do(lambda e: e.tensor_tensor(k["nr"], k["e1"], k["cs"], ALU.mult), p13)
        p13 = V.do(lambda e: e.tensor_tensor(k["nr"], k["nr"], k["hs"], ALU.subtract), p13)
        p14 = V.do(lambda e: e.tensor_tensor(k["ni"], k["r"], k["sn"], ALU.mult), p10)
        pd = V.do(lambda e: e.tensor_tensor(k["den"], lre, lre, ALU.mult))
        pe_ = V.do(lambda e: e.tensor_tensor(k["t1"], lim, lim, ALU.mult), p14)
        pd = V.do(lambda e: e.tensor_tensor(k["den"], k["den"], k["t1"], ALU.add), pe_)
        pd = V.do(lambda e: e.reciprocal(k["den"], k["den"]), pd)
        for name, (a, b, op) in {"cr": ("nr", "ni", ALU.add), "ci": ("ni", "nr", ALU.subtract)}.items():
            pd = V.do(lambda e, name=name, a=a: e.tensor_tensor(k[name], k[a], lre, ALU.mult), pd)
            pd = V.do(lambda e, b=b: e.tensor_tensor(k["t1"], k[b], lim, ALU.mult), pd)
            pd = V.do(lambda e, name=name, op=op: e.tensor_tensor(k[name], k[name], k["t1"], op), pd)
            pd = V.do(lambda e, name=name: e.tensor_tensor(k[name], k[name], k["den"], ALU.mult), pd)
        state["coef"] = pd
        yield
        read, stored = None, [None, None]
        for j in range(SJ):
            b = j % 2
            for s in range(3):
                p1 = V.do(lambda e, s=s, j=j: e.tensor_scalar(x[:, s, :], steps, k["ph"][:, j:j + 1], 0.25 * s, ALU.mult, ALU.add),
                          have_steps, p9, read)
            p2 = V.do(lambda e: e.tensor_scalar(w, x, HALF_UP, -HALF_UP, ALU.add, ALU.add), p1)
            p2 = V.do(lambda e: e.tensor_tensor(x, x, w, ALU.subtract), p2)
            read = S.do(lambda e, b=b: e.activation(out_bufs[b], x, ACT.Sin, scale=TWO_PI), p2, stored[b])
            stored[b] = store_trig[b].start(S, A["trig"][j], out_bufs[b], read)
            yield

    load_kept = Load(sem("stream_kept"))
    tables = [ssm_tables()]
    modulation_first()
    while tables:
        advance(tables)
    tables_done = [load.last() for load in store_trig]
    for q in (V, S, G, T):
        q.wait(*tables_done, V.last(), S.last())
    background.append(modulation_rest())
    for l in range(DEPTH):
        pre_norm(l)
        layer(l)

    ends = [q.last() for q in (V, S, G, T)]
    work_held.__exit__(None, None, None)
    feat_held.__exit__(None, None, None)
    h_t = h_t_words.rearrange("p (k t) -> p k t", t=T2)
    VK = 3 * P
    split_words = 2 * KT * T2 + 2 * (QL // P) * T2 + 2 * (KL // P) * VK
    x_held, x_r = tensor("split_inputs", split_words, F32R)
    at = 2 * KT * T2
    x_s = x_r[:, 0:at].rearrange("p (s k t) -> p s k t", s=2, k=KT)
    qa_s = x_r[:, at:at + 2 * (QL // P) * T2].rearrange("p (s k t) -> p s k t", s=2, k=QL // P)
    at += 2 * (QL // P) * T2
    kva_s = x_r[:, at:at + 2 * (KL // P) * VK].rearrange("p (s k t) -> p s k t", s=2, k=KL // P)
    O = Room(old_t, LT * D)
    k_nope = O.two(MH, T2)
    v_rows = [O.one(MH * HD)]
    scan_v = O.two(2, T2)
    k_pe = O.one(T2)
    O = Room(old_t, NT * D, LT * D)
    c_re, c_im = O.two(SJ, 32), O.two(SJ, 32)
    meta = old_t[0:META, O.at:O.at + D]
    v_rows += [O.one(MH * HD) for _ in range(2)]
    work_words = (NCONST2 + MH * TQ + MH // 2 * TQ + ST * T2 + 6 * 2 * T2 + 2 * 3 * T2 + 5 * T2 + 2 * T2 + 3 * P + T2
                  + (KL // P) * T2 + (QL // P) * T2 + 2 * ST * P)
    work_held, work_t = tensor("second_block_work", work_words)
    W = Room(work_t, work_words)
    block_consts[0] = W.one(NCONST2)
    q_nope_words = W.one(MH * TQ)
    q_nope = q_nope_words.rearrange("p (h t) -> p h t", t=TQ)
    q_pe = W.two(MH // 2, TQ)
    o_t = q_nope
    u_t = W.two(ST, T2)
    scan = {name: W.two(2, T2) for name in ("p1", "p2", "q1", "q2", "g", "h")}
    scan["v"] = scan_v
    trig_bufs = [W.two(3, T2) for _ in range(2)]
    norm_bufs = ([W.one(T2) for _ in range(2)], [W.one(T2) for _ in range(2)], W.one(T2))
    mp = [W.one(T2) for _ in range(2)]
    mpt = W.two(3, P)
    pe_tmp = W.one(T2)
    kva_t, qa_t = W.two(KL // P, T2), W.two(QL // P, T2)
    bt_re, bt_im = W.two(ST, P), W.two(ST, P)

    for q in (V, S, G, T):
        q.wait(*ends, *state["h"][0:LT])
    acc_banks[0] = 3
    h_lat = old_h[:, 0:LT, :]

    have_c2 = load_c.start(S, block_consts[0], A["consts_2"])
    for q in (V, G, T, S):
        q.wait(have_c2)
    load_meta, load_b = Load(sem("meta_loaded")), Load(sem("ssm_loaded"))
    have_meta = load_meta.start(S, meta, A["meta"])

    def raw_words(name):
        return scan[name].rearrange("p a b -> p (a b)")[:, 0:CH]
    raw_bre, raw_bim, raw_cre, raw_cim, tm, tm2 = (raw_words(n) for n in ("p1", "p2", "q1", "q2", "g", "h"))
    for dst, name in ((raw_bre, "b_re"), (raw_bim, "b_im"), (raw_cre, "c_re"), (raw_cim, "c_im")):
        have_b = load_b.start(S, dst, A[name])

    h_ready = []
    for f in range(KT):
        tb = banks[3 + f % 5]
        T.do(lambda e, f=f, tb=tb: e.transpose(tb[:, 0:META], meta[:, f * P:(f + 1) * P], ident[0:META, 0:META]),
             have_meta, tb.free, mark=False)
        for t in range(LT):
            p1 = T.do(lambda e, f=f, t=t, tb=tb: e.transpose(tb[:, META + t * P:META + (t + 1) * P],
                                                             h_lat[:, t, f * P:(f + 1) * P], ident), mark=t == 1)
        tb.free = copy_out(h_t[:, f, :], tb[:, 0:T2], p1)
        h_ready.append(tb.free)
    h_turned = p1

    sq_free, tmp_free = [None, None], [None, None]
    norm_cols = cols(3)
    rb_free, cols_free = [None], [None]

    def norm_rows(src, n, width, ready, gain, dst, d_f, t0, t1, free=None):
        sq, tmp, rb = norm_bufs
        w = t1 - t0
        sums_bank, tb, rbank = next_acc(), next_acc(), next_acc()
        for f in range(n):
            b = f % 2
            p1 = S.do(lambda e, f=f, b=b: e.activation(sq[b][:, 0:w], src[:, f, t0:t1], ACT.Square), ready[f], sq_free[b])
            sq_free[b] = T.do(lambda e, f=f, b=b: e.matmul(sums_bank[:, 0:w], ones, sq[b][:, 0:w], start=f == 0, stop=f == n - 1),
                              p1, sums_bank.free)
        r = rb[:, 0:w]
        sums_bank.free = p1 = V.do(lambda e: e.tensor_scalar(r, sums_bank[:, 0:w], 1.0 / width, EPS, ALU.mult, ALU.add),
                                   sq_free[b], rb_free[0])
        blocks_ = [(x, min(x + P, w)) for x in range(0, w, P)]
        for j, (x0, x1) in enumerate(blocks_):
            rb_free[0] = p2 = T.do(lambda e, j=j, x0=x0, x1=x1: e.transpose(tb[0:x1 - x0, j * P:(j + 1) * P], r[:, x0:x1], ident),
                                   p1, tb.free, mark=j == len(blocks_) - 1)
        for j, (x0, x1) in enumerate(blocks_):
            c = norm_cols[0:x1 - x0, j:j + 1]
            tb.free = p3 = V.do(lambda e, j=j, x0=x0, x1=x1, c=c: e.tensor_copy(c, tb[0:x1 - x0, j * P:j * P + 1]),
                                p2, cols_free[0])
            p4 = power(c, p3)
        for j, (x0, x1) in enumerate(blocks_):
            n_ = x1 - x0
            cols_free[0] = p5 = T.do(lambda e, j=j, x0=x0, x1=x1, n_=n_: e.matmul(
                rbank[:, x0:x1], norm_cols[0:n_, j:j + 1].broadcast_to((n_, P)), ident[0:n_, 0:n_], start=True, stop=True),
                p4, rbank.free, mark=j == len(blocks_) - 1)
        done = []
        for f in range(n):
            t = tmp[f % 2][:, 0:w]
            p6 = V.do(lambda e, f=f, t=t: e.scalar_tensor_tensor(
                out=t, in0=src[:, f, t0:t1], scalar=col(gain, f), in1=rbank[:, 0:w], op0=ALU.mult, op1=ALU.mult),
                p5, ready[f], tmp_free[f % 2])
            _, tmp_free[f % 2] = split_into(dst[:, 0, d_f + f, 0:w], dst[:, 1, d_f + f, 0:w], t, p6, free)
            done.append(tmp_free[f % 2])
        rbank.free = p6
        return done

    def j3(ap):
        return ap.rearrange("p (j c) -> p j c", c=16)
    blocks = q_nope_words[:, 0:2 * SJ * 32].rearrange("p (m j s c) -> p m j s c", m=2, j=SJ, s=2)
    z1 = G.do(lambda e: e.memset(q_nope_words, 0.0))
    crb, cib = bc(ssm_cr, 2, (P, SJ, 16)), bc(ssm_ci, 2, (P, SJ, 16))
    pd = None
    for m, (x1, x2, op) in enumerate(((raw_bre, raw_bim, ALU.subtract), (raw_bim, raw_bre, ALU.add))):
        pa = V.do(lambda e, x1=x1: e.tensor_tensor(j3(tm), j3(x1), crb, ALU.mult), have_b, state["coef"], pd)
        pb_ = V.do(lambda e, x2=x2: e.tensor_tensor(j3(tm2), j3(x2), cib, ALU.mult))
        for s in range(2):
            half = slice(s * SUB, (s + 1) * SUB)
            pd = V.do(lambda e, m=m, s=s, half=half, op=op: e.tensor_tensor(
                blocks[half, m, :, s, :], j3(tm[half]), j3(tm2[half]), op), pa, pb_, z1)
    b_ready = []
    for m, dst in enumerate((bt_re, bt_im)):
        for i in range(ST):
            if i % 4 == 0:
                tb = banks[3 + (2 * m + i // 4) % 4]
            src = blocks[:, m, 4 * i:4 * i + 4, :, :].rearrange("p j s c -> p (j s c)")
            p1 = T.do(lambda e, i=i, tb=tb, src=src: e.transpose(tb[:, (i % 4) * P:(i % 4 + 1) * P], src, ident),
                      pd, tb.free, mark=i % 4 == 3)
            if i % 4 == 3:
                tb.free = copy_out(dst[:, i - 3:i + 1, :], tb[:, :].rearrange("p (i q) -> p i q", q=P), p1)
                b_ready.append(tb.free)
    blocks_free = p1
    z2 = G.do(lambda e: e.memset(c_re, 0.0))
    z2 = G.do(lambda e: e.memset(c_im, 0.0))
    for s in range(2):
        half = slice(s * SUB, (s + 1) * SUB)
        V.do(lambda e, s=s, half=half: e.tensor_copy(c_re[half, :, s * 16:s * 16 + 16], j3(raw_cre[half])), z2, have_b)
        c_ready = V.do(lambda e, s=s, half=half: e.tensor_scalar(c_im[half, :, s * 16:s * 16 + 16], j3(raw_cim[half]),
                                                                 -1.0, None, ALU.mult))
    ssm_raw_free = c_ready

    xn = norm_rows(h_t, KT, D, h_ready, "mix_g", x_s, 0, 0, T2)

    def products(bank, hi, lo, kt, k0, last, x, x0, ready, t0, t1, *points):
        for k_ in range(kt):
            kk = k0 + k_
            cut = slice(k_ * P, (k_ + 1) * P)
            done = triple(bank[:, 0:t1 - t0], (hi[:, cut], lo[:, cut]), (x[:, 0, x0 + kk, t0:t1], x[:, 1, x0 + kk, t0:t1]),
                          kk == 0, kk == last, *points, bank.free, ready[kk], mark=k_ == kt - 1)
        return done

    def columns(pieces, x, x0, ready, t0, t1, bank):
        for g in range(pieces):
            hi, lo, here, i = take("split")
            split_free[i] = products(bank, hi, lo, 8, 8 * g, 8 * pieces - 1, x, x0, ready, t0, t1, here)
            side()
        return split_free[i]

    load_trig = [Load(sem(f"trig{i}_loaded")) for i in range(2)]
    u_ready, qa_ready, kva_ready, g_ready = [], [], [], []

    def scan_steps():
        p1_, p2_, q1_, q2_, v_, g_, h_ = (scan[n] for n in ("p1", "p2", "q1", "q2", "v", "g", "h"))
        bur_b, bui_b, yb = banks[3], banks[4], banks[7]
        trig_have, trig_free = {}, {}
        tmp_point = [ssm_raw_free]

        def load(j):
            if j < SJ:
                trig_have[j] = load_trig[j % 2].start(G, trig_bufs[j % 2], A["trig"][j], *tables_done, trig_free.get(j - 2))

        def rows(j):
            return slice(32 * (j % 4), 32 * (j % 4) + 32)
        load(0)
        load(1)
        in_done, v_read, v_done, h_done_, h_read = {}, {-1: pd}, {}, {}, {-1: pd}
        q_free = ssm_raw_free
        for step in range(SJ + 2):
            j = step
            if j < SJ:
                i = j // 4
                while len(u_ready) <= i:
                    yield
                tr = trig_bufs[j % 2]
                b1 = T.do(lambda e, i=i, j=j: e.matmul(bur_b[:, 0:T2], bt_re[rows(j), i, :], u_t[rows(j), i, :],
                                                       start=True, stop=True), u_ready[i], bur_b.free, *b_ready)
                b2 = T.do(lambda e, i=i, j=j: e.matmul(bui_b[:, 0:T2], bt_im[rows(j), i, :], u_t[rows(j), i, :],
                                                       start=True, stop=True), u_ready[i], bui_b.free)
                c1 = V.do(lambda e, tr=tr: e.tensor_tensor(p1_, bc(bur_b[:, 0:T2], 1, (P, 2, T2)), tr[:, 1:3, :], ALU.mult),
                          b1, trig_have[j], ssm_raw_free, tmp_point[0], v_done.get(j - 1))
                c2 = V.do(lambda e, tr=tr: e.tensor_tensor(p2_, bc(bui_b[:, 0:T2], 1, (P, 2, T2)), tr[:, 0:2, :], ALU.mult), b2)
                bur_b.free, bui_b.free = c1, c2
            j = step - 1
            if 0 <= j < SJ:
                rr = ssm_r[:, j:j + 1].broadcast_to((P, T2))
                s1 = V.do(lambda e, rr=rr: e.tensor_tensor_scan(g_[:, 0, :], rr, v_[:, 0, :], 0.0, ALU.mult, ALU.add), v_done[j],
                          trig_free.get(j - 1))
                s2 = V.do(lambda e, rr=rr: e.tensor_tensor_scan(g_[:, 1, :], rr, v_[:, 1, :], 0.0, ALU.mult, ALU.add))
                v_read[j] = s2
            if step < SJ:
                v_done[step] = G.do(lambda e: e.tensor_tensor(v_, p1_, p2_, ALU.add), c2, v_read[step - 1], h_turned)
            if 0 <= j < SJ:
                tr = trig_bufs[j % 2]
                e1 = V.do(lambda e, tr=tr: e.tensor_tensor(q1_, bc(g_[:, 0, :], 1, (P, 2, T2)), tr[:, 0:2, :], ALU.mult),
                          s1, q_free)
                e2 = V.do(lambda e, tr=tr: e.tensor_tensor(q2_, bc(g_[:, 1, :], 1, (P, 2, T2)), tr[:, 1:3, :], ALU.mult), s2)
                trig_free[j] = e2
                h_done_[j] = q_free = G.do(lambda e: e.tensor_tensor(h_, q1_, q2_, ALU.add), e2, h_read[j - 1])
                load(j + 2)
            yield
            if 0 <= j < SJ:
                i = j // 4
                T.do(lambda e, j=j: e.matmul(yb[rows(j), 0:T2], c_re[:, j, :], h_[:, 1, :], start=True, stop=False,
                                             tile_position=(0, rows(j).start)), h_done_[j], c_ready, yb.free, mark=False)
                y2 = T.do(lambda e, j=j: e.matmul(yb[rows(j), 0:T2], c_im[:, j, :], h_[:, 0, :], start=False, stop=True,
                                                  tile_position=(0, rows(j).start)))
                h_read[j] = y2
                if j % 4 == 3:
                    yy, tt_ = u_t[:, i, :], p1_[:, 0, :]
                    w = V.do(lambda e, i=i, yy=yy: e.scalar_tensor_tensor(out=yy, in0=yy, scalar=col("d_skip", i),
                                                                          in1=yb[:, 0:T2], op0=ALU.mult, op1=ALU.add), y2)
                    yb.free = w
                    w2 = S.do(lambda e, yy=yy: e.activation(tt_, yy, ACT.Square), w, v_done[min(step, SJ - 1)])
                    w2 = V.do(lambda e: e.tensor_scalar(tt_, tt_, 0.044715, 1.0, ALU.mult, ALU.add), w2)
                    w2 = V.do(lambda e, yy=yy: e.tensor_tensor(tt_, tt_, yy, ALU.mult), w2)
                    yield
                    w2 = S.do(lambda e: e.activation(tt_, tt_, ACT.Tanh, scale=math.sqrt(2.0 / math.pi)), w2)
                    w2 = V.do(lambda e: e.tensor_scalar(tt_, tt_, 1.0, 0.5, ALU.add, ALU.mult), w2)
                    tmp_point[0] = V.do(lambda e, yy=yy: e.tensor_tensor(yy, yy, tt_, ALU.mult), w2)
                    g_ready.append(tmp_point[0])

    side_work.append(scan_steps())
    for ct in range(15):
        bank = next_acc()
        done = columns(2, x_s, 0, xn, 0, T2, bank)
        dst = (u_t[:, ct, :] if ct < 8 else qa_t[:, ct - 8, :] if ct < 12 else kva_t[:, ct - 12, :] if ct < 14 else pe_tmp)
        bank.free = S.do(lambda e, dst=dst, bank=bank: e.activation(dst, bank[:, 0:T2], ACT.Copy), done)
        (u_ready if ct < 8 else qa_ready if ct < 12 else kva_ready).append(bank.free)
    x_used = done
    kpe_in = bank.free
    turn_tmp_free = [None]

    def turn_pe(src, dst, t0, ready, *points):
        w = T2 - t0
        bb = next_acc()
        a2 = T.do(lambda e: e.matmul(bb[:, 0:w], const("pe_turn"), src, start=True, stop=True), ready, bb.free)
        t = turn_tmp[:, 0:w]
        c1 = V.do(lambda e: e.tensor_tensor(dst, src, const("pe_cos")[:, t0:T2], ALU.mult), ready, *points)
        bb.free = c2 = V.do(lambda e: e.tensor_tensor(t, bb[:, 0:w], const("pe_sin")[:, t0:T2], ALU.mult), a2, turn_tmp_free[0])
        turn_tmp_free[0] = V.do(lambda e: e.tensor_tensor(dst, dst, t, ALU.add), c2, c1)
        return turn_tmp_free[0]

    turn_tmp = mp[1]
    kpe_ready = turn_pe(pe_tmp, k_pe, 0, kpe_in, h_turned)
    pe_tmp_free = kpe_ready
    qa_n = norm_rows(qa_t, QL // P, QL, qa_ready, "qa_g", qa_s, 0, 0, T2)
    kva_n = norm_rows(kva_t, KL // P, KL, kva_ready, "kva_g", kva_s, 0, 0, T2)
    fill = S.do(lambda e: e.activation(kva_s[:, :, :, T2:VK].rearrange("p s k t -> p (s k) t"),
                                       bc(ident[:, 0:VK - T2], 1, (P, 4, VK - T2)), ACT.Copy, scale=0.0))
    qn_ready, qp_ready = [], []
    for grp in range(6):
        hi, lo, here, i = take("split")
        for s in range(2):
            bank = next_acc()
            part = slice(s * CH, (s + 1) * CH)
            done = products(bank, hi[:, part], lo[:, part], 4, 0, 3, qa_s, 0, qa_n, Q0, T2, here)
            n = 2 * grp + s
            if n < MH:
                bank.free = S.do(lambda e, n=n, bank=bank: e.activation(q_nope[:, n, :], bank[:, 0:TQ], ACT.Copy), done, blocks_free)
                qn_ready.append(bank.free)
            else:
                src = pe_tmp[:, 0:TQ]
                bank.free = S.do(lambda e, bank=bank, src=src: e.activation(src, bank[:, 0:TQ], ACT.Copy), done, pe_tmp_free)
                pe_tmp_free = turn_pe(src, q_pe[:, n - MH, :], Q0, bank.free)
                qp_ready.append(pe_tmp_free)
            side()
        split_free[i] = done
    kn_ready = []
    for grp in range(2):
        hi, lo, here, i = take("split")
        for s in range(4):
            h = 4 * grp + s
            bank = next_acc()
            part = slice(s * 2 * P, (s + 1) * 2 * P)
            done = products(bank, hi[:, part], lo[:, part], 2, 0, 1, kva_s, 0, kva_n, 0, T2, here)
            bank.free = S.do(lambda e, h=h, bank=bank: e.activation(k_nope[:, h, :], bank[:, 0:T2], ACT.Copy), done, h_turned)
            kn_ready.append(bank.free)
            side()
        split_free[i] = done
    for c in range(2):
        hi, lo, here, i = take("split")
        for n in range(3):
            bank = next_acc()
            for k_ in range(2):
                cut = slice(k_ * CH, (k_ + 1) * CH)
                done = triple(bank[:, :], tuple(kva_s[:, s, k_, n * P:(n + 1) * P] for s in range(2)), (hi[:, cut], lo[:, cut]),
                              k_ == 0, k_ == 1, here, bank.free, kva_n[k_], fill, mark=k_ == 1)
            bank.free = S.do(lambda e, n=n, c=c, bank=bank: e.activation(v_rows[n][:, c * CH:(c + 1) * CH], bank[:, :], ACT.Copy),
                             done, h_turned)
            v_ready = bank.free
            side()
        split_free[i] = done

    mscale = 1.0 / math.sqrt(HD + SUB)
    mcols = [cols(4) for _ in range(4)]
    mp_free = [None, turn_tmp_free[0]]
    mpt_free = [None]
    o_ready = []
    mexp = [None] * 4
    tiles2 = [(2, P, META + P), (2 + P, P, T2), (0, 2, META)]
    units = [(h, n) for h in range(MH) for n in range(3)]
    att = {}

    def mla_scores(x):
        h, n = units[x]
        a, rows_, keys = tiles2[n]
        hp = slice((h % 2) * SUB, (h % 2) * SUB + SUB)
        u = x % 2
        m = mcols[x % 4]
        sb = banks[5]
        T.do(lambda e: e.matmul(sb[0:rows_, 0:keys], q_nope[:, h, a:a + rows_], k_nope[:, h, 0:keys], start=True, stop=False),
             qn_ready[h], kn_ready[h], sb.free, mark=False)
        p1 = T.do(lambda e: e.matmul(sb[0:rows_, 0:keys], q_pe[hp, h // 2, a:a + rows_], k_pe[hp, 0:keys], start=False, stop=True),
                  qp_ready[h // 2], kpe_ready)
        pr = mp[u][0:rows_, 0:keys]
        if rows_ == P:
            mask = const("mla_mask")[:, n * T2:n * T2 + keys]
            p2 = V.do(lambda e: e.scalar_tensor_tensor(out=pr, in0=sb[:, 0:keys], scalar=mscale, in1=mask,
                                                       op0=ALU.mult, op1=ALU.add), p1, mp_free[u])
        else:
            p2 = V.do(lambda e: e.tensor_scalar(pr, sb[0:rows_, 0:keys], mscale, None, ALU.mult), p1, mp_free[u])
        sb.free = p2
        mm = m[0:rows_]
        p3 = V.do(lambda e: e.tensor_reduce(mm[:, 0:1], pr, AX.X, ALU.max), p2, mexp[x % 4])
        p3 = V.do(lambda e: e.tensor_scalar(mm[:, 0:1], mm[:, 0:1], -1.0, None, ALU.mult), p3)
        mexp[x % 4] = p4 = S.do(lambda e: e.activation(pr, pr, ACT.Exp, bias=mm[:, 0:1], accum_out=mm[:, 1:2]), p3)
        p5 = V.do(lambda e: e.reciprocal(mm[:, 2:3], mm[:, 1:2]), p4)
        att[x] = V.do(lambda e: e.tensor_scalar(pr, pr, mm[:, 2:3], None, ALU.mult), p5)

    def mla_values(x):
        h, n = units[x]
        a, rows_, keys = tiles2[n]
        u = x % 2
        if n == 0:
            att["out"] = next_acc()
        ob = att["out"]
        pr = mp[u][0:rows_, 0:keys]
        tb = banks[6]
        kts = [(y, min(y + P, keys)) for y in range(0, keys, P)]
        for j, (x0, x1) in enumerate(kts):
            p6 = T.do(lambda e, j=j, x0=x0, x1=x1: e.transpose(tb[0:x1 - x0, j * P:j * P + rows_], pr[:, x0:x1],
                                                               ident[0:rows_, 0:rows_]), att[x], tb.free, mark=j == len(kts) - 1)
        mp_free[u] = p6
        for j, (x0, x1) in enumerate(kts):
            tb.free = p7 = S.do(lambda e, j=j, x0=x0, x1=x1: e.activation(
                mpt[0:x1 - x0, j, 0:rows_], tb[0:x1 - x0, j * P:j * P + rows_], ACT.Copy), p6, mpt_free[0])
        side()
        for j, (x0, x1) in enumerate(kts):
            p8 = T.do(lambda e, j=j, x0=x0, x1=x1: e.matmul(
                ob[:, a:a + rows_], v_rows[j][0:x1 - x0, h * HD:(h + 1) * HD], mpt[0:x1 - x0, j, 0:rows_],
                start=j == 0, stop=j == len(kts) - 1), p7, ob.free, v_ready, mark=j == len(kts) - 1)
        mpt_free[0] = p8
        if n == 2:
            ob.free = S.do(lambda e: e.activation(o_t[:, h, 0:TQ], ob[:, 0:TQ], ACT.Copy), p8)
            o_ready.append(ob.free)

    for x in range(len(units) + 1):
        if x < len(units):
            mla_scores(x)
        if x > 0:
            mla_values(x - 1)
    cat_o = norm_rows(o_t, ST, DS, o_ready, "attn_g", x_s, ST, 0, TQ, free=x_used)
    side_all()

    gs_ready = [split_into(x_s[:, 0, i, 0:TQ], x_s[:, 1, i, 0:TQ], u_t[:, i, Q0:T2], g_ready[i], x_used)[1] for i in range(ST)]
    ya_ready = []
    half_b = cols(ST)
    hb = V.do(lambda e: e.tensor_scalar(half_b, vec("b_glu"), 0.5, None, ALU.mult))
    glu_tmp, glu_free = [mp[0][:, 0:TQ], mp[1][:, 0:TQ]], list(mp_free)
    for ct in range(ST):
        bank = next_acc()
        done = columns(1, x_s, 0, gs_ready, 0, TQ, bank)
        d, y = glu_tmp[ct % 2], u_t[:, ct, Q0:T2]
        w1 = S.do(lambda e, d=d, ct=ct, bank=bank: e.activation(d, bank[:, 0:TQ], ACT.Tanh, scale=0.5, bias=half_b[:, ct:ct + 1]),
                  done, hb, glu_free[ct % 2])
        bank.free = w1
        w1 = V.do(lambda e, d=d: e.tensor_scalar(d, d, 1.0, 0.5, ALU.add, ALU.mult), w1)
        glu_free[ct % 2] = V.do(lambda e, d=d, y=y: e.tensor_tensor(y, y, d, ALU.mult), w1)
        ya_ready.append(glu_free[ct % 2])
    cat_y = norm_rows(u_t, ST, DS, ya_ready, "ssm_g", x_s, 0, Q0, T2, free=done)
    cat = cat_y + cat_o
    h2 = []
    for ct in range(KT):
        bank = next_acc()
        done = columns(2, x_s, 0, cat, 0, TQ, bank)
        bank.free = V.do(lambda e, ct=ct, bank=bank: e.tensor_tensor(h_t[:, ct, Q0:T2], h_t[:, ct, Q0:T2], bank[:, 0:TQ], ALU.add),
                         done, h_ready[ct])
        h2.append(bank.free)
    ends = [q.last() for q in (V, S, G, T)]
    work_held.__exit__(None, None, None)
    x_held.__exit__(None, None, None)
    old_held.__exit__(None, None, None)
    act_held, act_r = tensor("gated_split", 2 * FT * LAT, F32R)
    act_s = act_r[:, :].rearrange("p (s f t) -> p s f t", s=2, f=FT)
    ffn_words = 4 * LAT + 5 * TQ + LT * D
    _, ffn_t = tensor("ffn_work", ffn_words)
    W = Room(ffn_t, ffn_words)
    g_sb = [[W.one(LAT) for _ in range(2)] for _ in range(2)]
    sq, tmp_n, rb = [W.one(TQ) for _ in range(2)], [W.one(TQ) for _ in range(2)], W.one(TQ)
    h_rows = W.two(LT, D)
    xf_held, xf_r = tensor("ffn_input_split", 2 * KT * TQ, F32R)
    xf_s = xf_r[:, :].rearrange("p (s k t) -> p s k t", s=2, k=KT)
    for q in (V, S, G, T):
        q.wait(*ends)
    norm_bufs = (sq, tmp_n, rb)
    xf = norm_rows(h_t, KT, D, h2, "ffn_g", xf_s, 0, Q0, T2)
    acc_banks[0] = 4
    hr = {}
    for t in range(LT):
        for c in range(4):
            tb = banks[3 + (4 * t + c) % 4]
            for j in range(4):
                p1 = T.do(lambda e, t=t, c=c, j=j, tb=tb: e.transpose(
                    tb[:, j * P:(j + 1) * P], h_t[:, 4 * c + j, META + t * P:META + (t + 1) * P], ident),
                    h2[4 * c + j], tb.free, mark=j == 3)
            tb.free = copy_out(h_rows[:, t, c * CH:(c + 1) * CH], tb[:, :], p1)
            hr[(t, c)] = tb.free
    a_ready = []
    gfree = [None, None]
    for f in range(FT):
        bg, bv = banks[(2 * f) % 4], banks[(2 * f + 1) % 4]
        dg = columns(2, xf_s, 0, xf, 0, TQ, bg)
        dv = columns(2, xf_s, 0, xf, META - Q0, TQ, bv)
        u = f % 2
        a, b = g_sb[u]
        w0, w1, w2 = (col("conv_w", kk * FT + f) for kk in range(CONVW))
        p1 = S.do(lambda e, a=a, bg=bg, w2=w2, f=f: e.activation(a, bg[:, 2:2 + LAT], ACT.Identity, scale=w2, bias=col("conv_b", f)),
                  dg, gfree[u])
        p1 = V.do(lambda e, a=a, bg=bg, w1=w1: e.scalar_tensor_tensor(out=a, in0=bg[:, 1:1 + LAT], scalar=w1, in1=a,
                                                                     op0=ALU.mult, op1=ALU.add), p1)
        p1 = V.do(lambda e, a=a, bg=bg, w0=w0: e.scalar_tensor_tensor(out=a, in0=bg[:, 0:LAT], scalar=w0, in1=a,
                                                                     op0=ALU.mult, op1=ALU.add), p1)
        bg.free = p1
        p2 = S.do(lambda e, a=a, b=b: e.activation(b, a, ACT.Tanh, scale=0.5), p1, gfree[u])
        p2 = V.do(lambda e, a=a, b=b: e.scalar_tensor_tensor(out=b, in0=b, scalar=1.0, in1=a, op0=ALU.add, op1=ALU.mult), p2)
        p2 = V.do(lambda e, b=b, bv=bv: e.scalar_tensor_tensor(out=b, in0=bv[:, 0:LAT], scalar=0.5, in1=b,
                                                              op0=ALU.mult, op1=ALU.mult), p2, dv)
        bv.free = p2
        _, gfree[u] = split_into(act_s[:, 0, f, :], act_s[:, 1, f, :], b, p2)
        a_ready.append(gfree[u])
    xf_end = T.last()
    xf_held.__exit__(None, None, None)
    _, end_t = tensor("final_work", D + CH)
    fin_g, sc2 = end_t[:, 0:D], end_t[:, D:D + CH]
    S.wait(xf_end)
    load_fin = Load(sem("final_loaded"))
    have_fin = load_fin.start(S, fin_g, A["final_g"])
    store = Load(sem("stored"))
    ssf = cols(LT * 4)
    rsf = cols(LT)
    yd = {}
    for c in range(4):
        bk = [banks[4 + 2 * (c % 2)], banks[5 + 2 * (c % 2)]]
        for f in range(FT):
            k_ = f % KP
            if k_ == 0:
                hi, lo, here, i = take("split")
            w = (hi[:, k_ * CH:(k_ + 1) * CH], lo[:, k_ * CH:(k_ + 1) * CH])
            for t in range(LT):
                x = tuple(act_s[:, s, f, t * P:(t + 1) * P] for s in range(2))
                done = triple(bk[t][:, :], x, w, f == 0, f == FT - 1, here, bk[t].free, a_ready[f], mark=t == LT - 1)
            split_free[i] = done
        cut = slice(c * CH, (c + 1) * CH)
        for t in range(LT):
            p1 = V.do(lambda e, t=t, bk=bk, cut=cut: e.tensor_tensor(h_rows[:, t, cut], h_rows[:, t, cut], bk[t][:, :], ALU.add),
                      done, hr[(t, c)])
            bk[t].free = p1
            yd[(t, c)] = p1
            yd[("s", t)] = S.do(lambda e, t=t, cut=cut, c=c: e.activation(sc2, h_rows[:, t, cut], ACT.Square,
                                                                         accum_out=ssf[:, 4 * t + c:4 * t + c + 1]), p1, yd.get("sc"))
            yd["sc"] = yd[("s", t)]
    last = None
    for t in range(LT):
        r = rsf[:, t:t + 1]
        p1 = V.do(lambda e, t=t, r=r: e.tensor_reduce(r, ssf[:, 4 * t:4 * t + 4], AX.X, ALU.add), yd[("s", t)])
        p1 = V.do(lambda e, r=r: e.tensor_scalar(r, r, 1.0 / D, EPS, ALU.mult, ALU.add), p1)
        p1 = power(r, p1)
        for c in range(4):
            cut = slice(c * CH, (c + 1) * CH)
            p2 = V.do(lambda e, t=t, r=r, cut=cut: e.scalar_tensor_tensor(
                out=h_rows[:, t, cut], in0=h_rows[:, t, cut], scalar=r, in1=fin_g[:, cut], op0=ALU.mult, op1=ALU.mult),
                p1, have_fin, yd[("s", t)])
            last = store.start(Y, out[0, t * P:(t + 1) * P, cut], h_rows[:, t, cut], p2)
    Y.wait(last)

    with nc.Block() as block:
        @block.sync
        def _(e):
            Y.emit(e)

        @block.scalar
        def _(e):
            S.emit(e)

        @block.gpsimd
        def _(e):
            G.emit(e)

        @block.vector
        def _(e):
            V.emit(e)

        @block.tensor
        def _(e):
            T.emit(e)


def shape_constants():
    parts = [np.zeros((P, n), np.float32) for n in (NCONST, NCONST1, NCONST2)]

    def put(name, a):
        lo, hi = CONST[name]
        c = parts[0 if name in BOTH else 1 if name in FIRST_ONLY else 2]
        a = np.asarray(a, np.float32)
        c[:a.shape[0], lo:hi] = a.reshape(a.shape[0], hi - lo)
    put("ident", np.eye(P))
    put("ones", np.ones((P, P)))
    tok = np.arange(LAT)
    for name, dim in (("s", SUB), ("h", HD)):
        nf = dim // 4
        inv = (np.float32(10000.0) ** (-np.arange(nf, dtype=np.float32) / np.float32(nf))).astype(np.float32)
        row, col_ = (tok // GRID).astype(np.float32), (tok % GRID).astype(np.float32)
        ang = np.concatenate([row[:, None] * inv, col_[:, None] * inv], -1).astype(np.float32)
        for fn, what in ((np.cos, "cos_"), (np.sin, "sin_")):
            put(what + name, fn(ang).reshape(LT, P, -1).transpose(1, 0, 2))
    q, k = tok[:, None], tok[None, :]
    win = np.where(np.abs(k - q) <= 128, 0.0, MASKED)
    put("win_mask", win.reshape(LT, P, LAT).transpose(1, 0, 2))
    start = np.clip(q % GRID - 8, 0, GRID - 16)
    na = np.where((k % GRID >= start) & (k % GRID < start + 16), 0.0, MASKED)
    pos = np.arange(T2)
    chunk = np.where(pos < META, 0, 1 + (pos - META) // 64)
    mm = np.where(chunk[None, :] <= chunk[META:, None], 0.0, MASKED)
    put("mla_mask", mm.reshape(LT, P, T2).transpose(1, 0, 2))
    turn = np.zeros((64, 64), np.float32)
    for i in range(32):
        turn[32 + i, i] = -1.0
        turn[i, 32 + i] = 1.0
    both = np.zeros((P, P), np.float32)
    both[:64, :64] = turn
    both[64:, 64:] = turn
    put("pe_turn", both)
    inv = (1.0 / (np.float32(10000.0) ** (np.arange(0, 64, 2, dtype=np.float32) / np.float32(64)))).astype(np.float32)
    ang = (pos.astype(np.float32)[:, None] * inv[None, :]).astype(np.float32).T
    put("pe_cos", np.tile(np.cos(ang), (4, 1)))
    put("pe_sin", np.tile(np.sin(ang), (4, 1)))
    put("minus_half", np.full((P, 1), -0.5))
    na_mask = np.ascontiguousarray(na.reshape(LT, P, LAT).transpose(1, 0, 2).reshape(P, LT * LAT), np.float32)
    return *parts, na_mask, np.ascontiguousarray(np.broadcast_to(pos, (P, T2)), np.float32)


def lay_out(i):
    f = {n: np.asarray(a) for n, a in i.items()}

    def tiles(a):
        return a.reshape(-1, P).T
    parts = {
        "pre_g": tiles(f["pre_norm_g"].reshape(-1)), "post_g": tiles(f["post_norm_g"].reshape(-1)), "b_mod": tiles(f["b_mod"].reshape(-1)),
        "sink": np.broadcast_to(f["win_sink"].reshape(1, -1), (P, 2 * HEADS)),
        "silu_in": np.stack([tiles(f["c"][0]), tiles(f["c_ctx"])], -1).reshape(P, -1),
        "mix_g": tiles(f["mix_norm_2"][0]), "ffn_g": tiles(f["ffn_norm_2"][0]), "b_glu": tiles(f["b_glu_2"][0]),
        "d_skip": tiles(f["d_skip_2"][0]), "qa_g": tiles(f["q_a_norm_2"][0]), "kva_g": tiles(f["kv_a_norm_2"][0]),
        "ssm_g": tiles(f["out_norm_ssm_2"][0]), "attn_g": tiles(f["out_norm_attn_2"][0]),
        "conv_w": tiles(f["conv_w_2"][0].reshape(-1)), "conv_b": tiles(f["conv_b_2"][0]),
        "lam_re": tiles(f["lam_re_2"][0].reshape(-1)), "lam_im": tiles(f["lam_im_2"][0].reshape(-1)),
        "log_dt": tiles(np.repeat(f["log_dt_2"][0], SUB)),
    }
    vectors = np.concatenate([parts[n] for n in VEC], 1)

    def moving(w, n):
        return w.reshape(-1, KP, P, n, CH).transpose(3, 0, 2, 1, 4).reshape(n, -1, P, PIECE)

    def still(w, kg):
        return w.reshape(-1, kg, P, w.shape[1] // P, P).transpose(3, 0, 2, 1, 4).reshape(w.shape[1] // P, -1, P, kg * P)

    def gather(w, kg):
        n = PIECE // (kg * P)
        return w.reshape(kg, P, -1, n, P).transpose(2, 1, 3, 0, 4).reshape(-1, P, PIECE)
    tok = np.arange(LAT)
    q, k = tok[:, None], tok[None, :]
    rpb = f["na_rpb"]
    bias = rpb[:, :, (k // GRID) - (q // GRID) + 7, np.clip(k % GRID - q % GRID + 15, 0, 30)]
    w_q = f["w_q_b_2"][0].reshape(QL, MH, 192)
    w_q = np.concatenate([w_q[:, :, :P].reshape(QL, -1), w_q[:, :, P:].reshape(QL, -1)], 1)
    w_kv = f["w_kv_b_2"][0].reshape(KL, MH, 256)
    w2 = f["w_in_2"][0]
    down = f["w_down_2"][0]
    kpe = w2[:, 14 * P:]
    consts, consts_1, consts_2, na_mask, steps = shape_constants()
    a = {
        "vectors": vectors, "consts": consts, "consts_1": consts_1, "consts_2": consts_2, "na_mask": na_mask, "steps": steps,
        "x": f["x"][0].reshape(LT, P, D).transpose(1, 0, 2), "ctx": f["ctx"][0].reshape(LT, P, D).transpose(1, 0, 2),
        "meta": f["meta_tokens_2"],
        "w_mod": moving(f["w_mod"][0][:, :2 * D], 2 * MODC // 3),
        "w_mod_rows": f["w_mod"].reshape(DEPTH, KT, P, MODC, CH).transpose(0, 3, 1, 2, 4),
        "w_in": np.stack([moving(w, INC) for w in f["w_in"]]),
        "w_out": np.stack([moving(w, 4) for w in f["w_out"]]),
        "lambda_in": np.broadcast_to(np.stack([f["diff_lambda_q1"], f["diff_lambda_k1"], f["diff_lambda_q2"],
                                               f["diff_lambda_k2"]], 1).reshape(DEPTH, 1, -1), (DEPTH, P, 4 * SUB)),
        "subln": np.broadcast_to(f["diff_subln_g"][:, None], (DEPTH, P, HD)),
        "qk_g": np.broadcast_to(np.stack([f["qk_q_norm_g"], f["qk_k_norm_g"]], 1)[:, None], (DEPTH, P, 2, HD)),
        "na_bias": bias.reshape(DEPTH, HEADS, LT, P, LAT).transpose(0, 3, 1, 2, 4).reshape(DEPTH, P, HEADS * LT, LAT),
        "w_in2": still(w2[:, :14 * P], 8), "w_kpe": still(np.concatenate([kpe, kpe], 1), 8),
        "w_q": gather(w_q, QL // P),
        "w_kn": gather(w_kv[:, :, :P].reshape(KL, -1), KL // P), "w_v": moving(w_kv[:, :, P:].reshape(KL, -1), 2),
        "w_glu": gather(f["w_glu_2"][0], DS // P),
        "w_out2": still(f["w_out_2"][0], 8), "w_up": still(f["w_up_2"][0], 8),
        "w_down": moving(down[:(FT - 1) * P], 4),
        "w_down_end": down[(FT - 1) * P:].reshape(P, 4, CH).transpose(1, 0, 2),
        "b_re": f["b_re_2"][0].reshape(SJ, P, 16).transpose(1, 0, 2).reshape(P, CH),
        "b_im": f["b_im_2"][0].reshape(SJ, P, 16).transpose(1, 0, 2).reshape(P, CH),
        "c_re": f["c_re_2"][0].reshape(SJ, 2, 16, SUB).transpose(1, 3, 0, 2).reshape(P, CH),
        "c_im": f["c_im_2"][0].reshape(SJ, 2, 16, SUB).transpose(1, 3, 0, 2).reshape(P, CH),
        "final_g": np.broadcast_to(f["final_norm_2"][None], (P, D)),
    }
    return {n: np.ascontiguousarray(x) for n, x in a.items()}


def scratch_tensors(nc):
    shapes = {"kept_stream": (P, LT, D), "trig": (SJ, P, 3, T2)}
    return {n: nc.dram_tensor(n, shape, F32, kind="Internal").ap() for n, shape in shapes.items()}


def kernel(**inputs):
    import concourse.bacc as bacc
    from concourse.bass_utils import run_bass_kernel_spmd as run

    nc = bacc.Bacc("TRN2", target_bir_lowering=False, num_devices=1)
    arrays = lay_out(inputs)
    aps = {n: nc.dram_tensor(n, a.shape, mybir.dt.from_np(a.dtype), kind="ExternalInput").ap() for n, a in arrays.items()}
    out = nc.dram_tensor("out", (1, LAT, D), F32, kind="ExternalOutput").ap()
    aps.update(scratch_tensors(nc))
    build(nc, aps, out)
    r = run(nc, [arrays], core_ids=[0])
    return r.results[0]["out"]
```
